# Optimizing a Trainium2 kernel written in Bass

```python
import math
import jax, jax.numpy as jnp
from jax import lax
import numpy as np

D_MODEL = 1024
BATCH = 1
SEQ = 512
DEPTH = 1

CTX_LEN = 256
GRID_W = 64
W_R = 1280
H_R = 5
BW = W_R // H_R
LRU_C = 8.0
CONV_R = 4
CONV_R_LEFT = 2
W_G = 1024
H_G = 8
GC = W_G // H_G
CHUNK = 128
D_FF = 2816
N_MOD = 6
EPS = 1e-6
OFF_RX = 0
OFF_RG = OFF_RX + W_R
OFF_U = OFF_RG + W_R
OFF_V = OFF_U + W_G
OFF_GR = OFF_V + W_G
OFF_GG = OFF_GR + D_MODEL
N_IN = OFF_GG + D_MODEL


def _rmsnorm(x, g):
    xf = x.astype(jnp.float32)
    y = xf * lax.rsqrt(jnp.mean(xf * xf, axis=-1, keepdims=True) + EPS)
    return (y * g.astype(jnp.float32)).astype(x.dtype)

def _modulate(x, g, shift, scale):
    return _rmsnorm(x, g) * (1.0 + scale) + shift

def _dwconv1d(x, w, b):
    C = x.shape[-1]
    y = lax.conv_general_dilated(x, w[:, None, :], window_strides=(1,),
                                 padding=[(CONV_R_LEFT, CONV_R - 1 - CONV_R_LEFT)],
                                 dimension_numbers=('NWC', 'WIO', 'NWC'),
                                 feature_group_count=C)
    return y + b

def _dwconv2d(x, w, b):
    C = x.shape[-1]
    y = lax.conv_general_dilated(x, w[:, :, None, :], window_strides=(1, 1),
                                 padding=[(1, 1), (1, 1)],
                                 dimension_numbers=('NHWC', 'HWIO', 'NHWC'),
                                 feature_group_count=C)
    return y + b

def _linear_scan(a, b, h0, reverse):
    def step(h, ab):
        a_t, b_t = ab
        h = a_t * h + b_t
        return h, h
    h_last, hs = lax.scan(step, h0, (jnp.swapaxes(a, 0, 1), jnp.swapaxes(b, 0, 1)), reverse=reverse)
    return jnp.swapaxes(hs, 0, 1), h_last

def _rglru_dir(xr, lam, wa, ba, wx, bx, h0, reverse):
    B, T, _ = xr.shape
    xh = xr.reshape(B, T, H_R, BW)
    r = jax.nn.sigmoid(jnp.einsum('bthi,hij->bthj', xh, wa).reshape(B, T, W_R) + ba)
    i = jax.nn.sigmoid(jnp.einsum('bthi,hij->bthj', xh, wx).reshape(B, T, W_R) + bx)
    log_a = (-LRU_C * r * jax.nn.softplus(-lam)).astype(jnp.float32)
    a = jnp.exp(log_a)
    mult = jnp.sqrt(-jnp.expm1(2.0 * log_a))
    bt = mult * (i * xr).astype(jnp.float32)
    hs, h_last = _linear_scan(a, bt, h0, reverse)
    return hs.astype(xr.dtype), h_last

def _rglru_bidir(xr, lam, wa, ba, wx, bx, h0_f, h0_b):
    y_f, h_f = _rglru_dir(xr, lam[0], wa[0], ba[0], wx[0], bx[0], h0_f, False)
    y_b, h_b = _rglru_dir(xr, lam[1], wa[1], ba[1], wx[1], bx[1], h0_b, True)
    return y_f + y_b, h_f, h_b

def _chunk_mlp(u_raw, v_raw, g_v, w_s, b_s):
    B, T, _ = u_raw.shape
    u = jax.nn.gelu(u_raw)
    v = _rmsnorm(jax.nn.gelu(v_raw), g_v).reshape(B, T // CHUNK, CHUNK, H_G, GC)
    s = jnp.einsum('hpq,bnqhc->bnphc', w_s, v) + b_s[None, None, :, :, None]
    return u * s.reshape(B, T, W_G)

def _mixer_out(p, y_lru, g_v, w_s, b_s, w_pr, w_pg, w_out):
    y_r = jax.nn.gelu(p[..., OFF_RG:OFF_RG + W_R]) * y_lru
    y_g = _chunk_mlp(p[..., OFF_U:OFF_U + W_G], p[..., OFF_V:OFF_V + W_G], g_v, w_s, b_s)
    gate_r = jax.nn.sigmoid(p[..., OFF_GR:OFF_GR + D_MODEL])
    gate_g = jax.nn.sigmoid(p[..., OFF_GG:OFF_GG + D_MODEL])
    merged = gate_r * (y_r @ w_pr) + gate_g * (y_g @ w_pg)
    return merged @ w_out

def _conv_ffn(h, w_up, cw, cb, w_down, grid_h, grid_w):
    B, T, _ = h.shape
    up = h @ w_up
    g = _dwconv2d(up[..., :D_FF].reshape(B, grid_h, grid_w, D_FF), cw, cb).reshape(B, T, D_FF)
    return (jax.nn.gelu(g) * up[..., D_FF:]) @ w_down

def first_inputs(seed: int = 0) -> dict:
    key = jax.random.key(seed)
    ks = jax.random.split(key, 32)
    f32 = jnp.float32

    def nrm(k, shape, fan_in, gain=1.0):
        return (gain * fan_in ** -0.5) * jax.random.normal(k, shape, f32)

    u = jax.random.uniform(ks[8], (DEPTH, 2, W_R), f32, minval=0.9, maxval=0.999)
    a1 = u ** (1.0 / LRU_C)
    lru_lam = jnp.log(a1) - jnp.log1p(-a1)
    return {
        "x": jax.random.normal(ks[0], (BATCH, SEQ, D_MODEL), f32),
        "c": jax.random.normal(ks[1], (BATCH, D_MODEL), f32),
        "ctx": jax.random.normal(ks[2], (BATCH, CTX_LEN, D_MODEL), f32),
        "c_ctx": jax.random.normal(ks[3], (D_MODEL,), f32),
        "w_mod": nrm(ks[4], (DEPTH, D_MODEL, N_MOD * D_MODEL), D_MODEL, 0.5),
        "b_mod": 0.02 * jax.random.normal(ks[5], (DEPTH, N_MOD * D_MODEL), f32),
        "g_norm1": 1.0 + 0.02 * jax.random.normal(ks[6], (DEPTH, D_MODEL), f32),
        "w_in": nrm(ks[7], (DEPTH, D_MODEL, N_IN), D_MODEL),
        "conv_w": nrm(ks[9], (DEPTH, CONV_R, W_R), CONV_R),
        "conv_b": 0.02 * jax.random.normal(ks[10], (DEPTH, W_R), f32),
        "lru_lam": lru_lam,
        "lru_wa": nrm(ks[11], (DEPTH, 2, H_R, BW, BW), BW),
        "lru_ba": 0.02 * jax.random.normal(ks[12], (DEPTH, 2, W_R), f32),
        "lru_wx": nrm(ks[13], (DEPTH, 2, H_R, BW, BW), BW),
        "lru_bx": 0.02 * jax.random.normal(ks[14], (DEPTH, 2, W_R), f32),
        "g_v": 1.0 + 0.02 * jax.random.normal(ks[15], (DEPTH, W_G), f32),
        "w_s": nrm(ks[16], (DEPTH, H_G, CHUNK, CHUNK), CHUNK),
        "b_s": 1.0 + 0.02 * jax.random.normal(ks[17], (DEPTH, CHUNK, H_G), f32),
        "w_pr": nrm(ks[18], (DEPTH, W_R, D_MODEL), W_R),
        "w_pg": nrm(ks[19], (DEPTH, W_G, D_MODEL), W_G),
        "w_out": nrm(ks[20], (DEPTH, D_MODEL, D_MODEL), D_MODEL),
        "g_norm2": 1.0 + 0.02 * jax.random.normal(ks[21], (DEPTH, D_MODEL), f32),
        "w_up": nrm(ks[22], (DEPTH, D_MODEL, 2 * D_FF), D_MODEL),
        "ffn_conv_w": nrm(ks[23], (DEPTH, 3, 3, D_FF), 9.0),
        "ffn_conv_b": 0.02 * jax.random.normal(ks[24], (DEPTH, D_FF), f32),
        "w_down": nrm(ks[25], (DEPTH, D_FF, D_MODEL), D_FF),
        "g_final": 1.0 + 0.02 * jax.random.normal(ks[26], (D_MODEL,), f32),
    }

def first_block(x, c, ctx, c_ctx, w_mod, b_mod, g_norm1, w_in, conv_w, conv_b, lru_lam,
              lru_wa, lru_ba, lru_wx, lru_bx, g_v, w_s, b_s, w_pr, w_pg, w_out,
              g_norm2, w_up, ffn_conv_w, ffn_conv_b, w_down, g_final):
    B, T, _ = x.shape
    rows = T // GRID_W
    t_ctx = ctx.shape[1]
    for l in range(DEPTH):
        last = l == DEPTH - 1
        m_x = (jax.nn.silu(c) @ w_mod[l] + b_mod[l]).reshape(B, N_MOD, 1, D_MODEL)
        m_c = (jax.nn.silu(c_ctx) @ w_mod[l] + b_mod[l]).reshape(N_MOD, D_MODEL)
        lru = (lru_lam[l], lru_wa[l], lru_ba[l], lru_wx[l], lru_bx[l])
        gmlp_and_merge = (g_v[l], w_s[l], b_s[l], w_pr[l], w_pg[l], w_out[l])

        hc = _modulate(ctx, g_norm1[l], m_c[0], m_c[1])
        pc = hc @ w_in[l][:, :(W_R if last else N_IN)]
        xr_c = _dwconv1d(pc[..., OFF_RX:OFF_RX + W_R], conv_w[l], conv_b[l])
        h0 = jnp.zeros((B, W_R), jnp.float32)
        yc_lru, hc_f, hc_b = _rglru_bidir(xr_c, *lru, h0, h0)

        hx = _modulate(x, g_norm1[l], m_x[:, 0], m_x[:, 1])
        px = hx @ w_in[l]
        xr_x = _dwconv1d(px[..., OFF_RX:OFF_RX + W_R], conv_w[l], conv_b[l])
        yx_lru, _, _ = _rglru_bidir(xr_x, *lru, hc_f, hc_b)
        x = x + m_x[:, 2] * _mixer_out(px, yx_lru, *gmlp_and_merge)
        if not last:
            ctx_mid = ctx + m_c[2] * _mixer_out(pc, yc_lru, *gmlp_and_merge)

        h2 = _modulate(x, g_norm2[l], m_x[:, 3], m_x[:, 4])
        x = x + m_x[:, 5] * _conv_ffn(h2, w_up[l], ffn_conv_w[l], ffn_conv_b[l], w_down[l], rows, GRID_W)
        if not last:
            h2c = _modulate(ctx_mid, g_norm2[l], m_c[3], m_c[4])
            ctx = ctx_mid + m_c[5] * _conv_ffn(h2c, w_up[l], ffn_conv_w[l], ffn_conv_b[l], w_down[l], 1, t_ctx)
    return _rmsnorm(x, g_final)


_first_inputs = first_inputs


def first_inputs(seed=0):
    import zlib

    import numpy as np

    out = dict(_first_inputs(seed))
    spreads = {}
    factors = {'g_norm1': 6.543,
     'lru_ba': 8.0,
     'lru_bx': 8.0,
     'g_v': 8.0,
     'b_s': 8.0,
     'g_norm2': 8.0,
     'ffn_conv_b': 8.0,
     'g_final': 2.802}
    for name, (base, spread) in spreads.items():
        noise = np.random.default_rng([zlib.crc32(name.encode()), seed]).standard_normal(out[name].shape)
        drawn = base * np.exp(spread * noise) if base else spread * noise
        out[name] = __import__('jax').numpy.asarray(drawn.astype(out[name].dtype))
    for name, factor in factors.items():
        out[name] = (out[name] * factor).astype(out[name].dtype)
    return out


_narrow_inputs = first_inputs


def first_inputs(seed=0):

    out = dict(_narrow_inputs(seed))
    wider = {'conv_b': 3.97,
     'lru_ba': 5.23,
     'lru_bx': 4.39,
     'g_v': 4.35,
     'b_s': 4.45,
     'ffn_conv_b': 4.21,
     'g_final': 3.14}
    for name, times in wider.items():
        mean = out[name].mean()
        out[name] = (mean + times * (out[name] - mean)).astype(out[name].dtype)
    return out


CHUNK_2 = 64

SSM_WIDTH = 512
SSM_GROUP = 16
SSM_GROUPS = SSM_WIDTH // SSM_GROUP
SSM_STATE = 64
DT_MIN = 1e-3
DT_MAX = 1e-1

ATT_HEADS = 8
HEAD_DIM = 128
ATT_WIDTH = ATT_HEADS * HEAD_DIM
Q_BLOCK = 128

N_BRANCHES = 2
IN_SPLITS = (
    SSM_WIDTH,
    SSM_WIDTH + ATT_WIDTH,
    SSM_WIDTH + 2 * ATT_WIDTH,
    SSM_WIDTH + 3 * ATT_WIDTH,
    SSM_WIDTH + 3 * ATT_WIDTH + ATT_HEADS,
    SSM_WIDTH + 3 * ATT_WIDTH + ATT_HEADS + D_MODEL,
)
IN_COLS = SSM_WIDTH + 3 * ATT_WIDTH + ATT_HEADS + N_BRANCHES * D_MODEL

PEER_HEADS = 8
PEER_KEYS = 128
PEER_EXPERTS = PEER_KEYS * PEER_KEYS
PEER_QUERY = 256
PEER_HALF = PEER_QUERY // 2
PEER_TOPK = 16
TOKEN_BLOCK = 128


def rms_norm(x, g):
    x32 = x.astype(jnp.float32)
    y = x32 * lax.rsqrt(jnp.mean(x32 * x32, axis=-1, keepdims=True) + EPS)
    return (y * g.astype(jnp.float32)).astype(x.dtype)

def _complex_affine_combine(earlier, later):
    ar1, ai1, br1, bi1 = earlier
    ar2, ai2, br2, bi2 = later
    return (ar2 * ar1 - ai2 * ai1,
            ar2 * ai1 + ai2 * ar1,
            ar2 * br1 - ai2 * bi1 + br2,
            ar2 * bi1 + ai2 * br1 + bi2)

def s5_branch(u, a_re, a_im, log_step, b_re, b_im, c_re, c_im, d_skip, w_glu):
    bsz, seq = u.shape[0], u.shape[1]
    f32 = jnp.float32
    u32 = u.astype(f32)
    ug = u32.reshape(bsz, seq, SSM_GROUPS, SSM_GROUP)
    step = jnp.exp(log_step.astype(f32))[:, None]
    ar = a_re.astype(f32)
    ai = a_im.astype(f32)
    mag = jnp.exp(ar * step)
    lam_re = mag * jnp.cos(ai * step)
    lam_im = mag * jnp.sin(ai * step)
    nr = lam_re - 1.0
    ni = lam_im
    den = ar * ar + ai * ai
    coef_re = (nr * ar + ni * ai) / den
    coef_im = (ni * ar - nr * ai) / den
    br = coef_re[..., None] * b_re.astype(f32) - coef_im[..., None] * b_im.astype(f32)
    bi = coef_re[..., None] * b_im.astype(f32) + coef_im[..., None] * b_re.astype(f32)
    xr = jnp.einsum('blgh,gph->blgp', ug, br)
    xi = jnp.einsum('blgh,gph->blgp', ug, bi)
    lr = jnp.broadcast_to(lam_re[None, None], (1, seq, SSM_GROUPS, SSM_STATE))
    li = jnp.broadcast_to(lam_im[None, None], (1, seq, SSM_GROUPS, SSM_STATE))
    _, _, sr, si = lax.associative_scan(_complex_affine_combine, (lr, li, xr, xi), axis=1)
    y = (jnp.einsum('blgp,ghp->blgh', sr, c_re.astype(f32))
         - jnp.einsum('blgp,ghp->blgh', si, c_im.astype(f32)))
    y = y.reshape(bsz, seq, SSM_WIDTH) + d_skip.astype(f32) * u32
    y = jax.nn.gelu(y).astype(u.dtype)
    z = y @ w_glu
    val, gate = jnp.split(z, 2, axis=-1)
    return val * jax.nn.sigmoid(gate)

def head_rms_norm(x, g):
    x32 = x.astype(jnp.float32)
    y = x32 * lax.rsqrt(jnp.mean(x32 * x32, axis=-1, keepdims=True) + EPS)
    return (y * g.astype(jnp.float32)).astype(x.dtype)

def forgetting_attention(q, k, v, f_logit, f_bias, q_g, k_g):
    bsz, seq = q.shape[0], q.shape[1]
    q = head_rms_norm(q.reshape(bsz, seq, ATT_HEADS, HEAD_DIM), q_g).transpose(0, 2, 1, 3)
    k = head_rms_norm(k.reshape(bsz, seq, ATT_HEADS, HEAD_DIM), k_g).transpose(0, 2, 1, 3)
    v = v.reshape(bsz, seq, ATT_HEADS, HEAD_DIM).transpose(0, 2, 1, 3)
    log_f = jax.nn.log_sigmoid((f_logit + f_bias).astype(jnp.float32)).transpose(0, 2, 1)
    cum = jnp.cumsum(log_f, axis=-1)
    n_blk = seq // Q_BLOCK
    q_blocks = q.reshape(bsz, ATT_HEADS, n_blk, Q_BLOCK, HEAD_DIM).transpose(2, 0, 1, 3, 4)
    c_blocks = cum.reshape(bsz, ATT_HEADS, n_blk, Q_BLOCK).transpose(2, 0, 1, 3)
    key_pos = jnp.arange(seq)
    scale = HEAD_DIM ** -0.5

    def one_block(args):
        blk, q_blk, c_blk = args
        s = jnp.einsum('bhqd,bhkd->bhqk', q_blk, k).astype(jnp.float32) * scale
        s = s + c_blk[..., None] - cum[:, :, None, :]
        q_pos = blk * Q_BLOCK + jnp.arange(Q_BLOCK)
        s = jnp.where(key_pos[None, :] <= q_pos[:, None], s, -jnp.inf)
        p = jax.nn.softmax(s, axis=-1)
        return jnp.einsum('bhqk,bhkd->bhqd', p.astype(v.dtype), v)

    o = lax.map(one_block, (jnp.arange(n_blk), q_blocks, c_blocks))
    return o.transpose(1, 0, 3, 2, 4).reshape(bsz, seq, ATT_WIDTH)

def peer_ffn(h, w_query, sub_keys, u_tab, v_tab):
    bsz, seq, d = h.shape
    q = (h @ w_query).reshape(bsz, seq, PEER_HEADS, 2, PEER_HALF).astype(jnp.float32)
    scores = jnp.einsum('blhcd,hckd->blhck', q, sub_keys.astype(jnp.float32))
    s_top, i_top = lax.top_k(scores, PEER_TOPK)
    cand_s = (s_top[..., 0, :, None] + s_top[..., 1, None, :]).reshape(bsz, seq, PEER_HEADS, PEER_TOPK * PEER_TOPK)
    cand_i = (i_top[..., 0, :, None] * PEER_KEYS + i_top[..., 1, None, :]).reshape(bsz, seq, PEER_HEADS, PEER_TOPK * PEER_TOPK)
    best_s, pos = lax.top_k(cand_s, PEER_TOPK)
    expert_idx = jnp.take_along_axis(cand_i, pos, axis=-1)
    gates = jax.nn.softmax(best_s, axis=-1)
    n_tok = bsz * seq
    n_tb = n_tok // TOKEN_BLOCK
    h_blocks = h.reshape(n_tb, TOKEN_BLOCK, d)
    i_blocks = expert_idx.reshape(n_tb, TOKEN_BLOCK, PEER_HEADS, PEER_TOPK)
    g_blocks = gates.reshape(n_tb, TOKEN_BLOCK, PEER_HEADS, PEER_TOPK)

    def one_block(args):
        h_blk, i_blk, g_blk = args
        u_sel = u_tab[i_blk]
        act = jax.nn.gelu(jnp.einsum('td,thkd->thk', h_blk, u_sel).astype(jnp.float32))
        w = (g_blk * act).astype(h.dtype)
        return jnp.einsum('thk,thkd->td', w, v_tab[i_blk])

    out = lax.map(one_block, (h_blocks, i_blocks, g_blocks))
    return out.reshape(bsz, seq, d)

def second_inputs(seed: int = 0) -> dict:
    key = jax.random.key(seed)
    ks = jax.random.split(key, 21)
    f32 = jnp.float32
    nrm = lambda k, shape: jax.random.normal(k, shape, dtype=f32)
    x = nrm(ks[0], (BATCH, SEQ, D_MODEL))
    mix_norm_g = 1.0 + 0.02 * nrm(ks[1], (DEPTH, D_MODEL))
    w_in = nrm(ks[2], (DEPTH, D_MODEL, IN_COLS)) * D_MODEL ** -0.5
    ssm_a_re = -0.5 + 0.01 * nrm(ks[3], (DEPTH, SSM_GROUPS, SSM_STATE))
    ssm_a_im = math.pi * jnp.arange(SSM_STATE, dtype=f32) + 0.01 * nrm(ks[4], (DEPTH, SSM_GROUPS, SSM_STATE))
    ssm_log_step = jax.random.uniform(ks[5], (DEPTH, SSM_GROUPS), dtype=f32, minval=math.log(DT_MIN), maxval=math.log(DT_MAX))
    ssm_b_re = nrm(ks[6], (DEPTH, SSM_GROUPS, SSM_STATE, SSM_GROUP)) * (2.0 * SSM_GROUP) ** -0.5
    ssm_b_im = nrm(ks[7], (DEPTH, SSM_GROUPS, SSM_STATE, SSM_GROUP)) * (2.0 * SSM_GROUP) ** -0.5
    ssm_c_re = nrm(ks[8], (DEPTH, SSM_GROUPS, SSM_GROUP, SSM_STATE)) * (2.0 * SSM_STATE) ** -0.5
    ssm_c_im = nrm(ks[9], (DEPTH, SSM_GROUPS, SSM_GROUP, SSM_STATE)) * (2.0 * SSM_STATE) ** -0.5
    ssm_d = nrm(ks[10], (DEPTH, SSM_WIDTH))
    ssm_w_glu = nrm(ks[11], (DEPTH, SSM_WIDTH, 2 * D_MODEL)) * SSM_WIDTH ** -0.5
    fox_forget_bias = 2.0 + 0.5 * nrm(ks[12], (DEPTH, ATT_HEADS))
    q_norm_g = 1.0 + 0.02 * nrm(ks[13], (DEPTH, HEAD_DIM))
    k_norm_g = 1.0 + 0.02 * nrm(ks[14], (DEPTH, HEAD_DIM))
    w_out = nrm(ks[15], (DEPTH, D_MODEL, D_MODEL)) * D_MODEL ** -0.5
    ffn_norm_g = 1.0 + 0.02 * nrm(ks[16], (DEPTH, D_MODEL))
    peer_w_query = nrm(ks[17], (DEPTH, D_MODEL, PEER_HEADS * PEER_QUERY)) * D_MODEL ** -0.5
    peer_sub_keys = nrm(ks[18], (DEPTH, PEER_HEADS, 2, PEER_KEYS, PEER_HALF)) * PEER_HALF ** -0.5
    peer_u = nrm(ks[19], (DEPTH, PEER_EXPERTS, D_MODEL)) * D_MODEL ** -0.5
    peer_v = nrm(ks[20], (DEPTH, PEER_EXPERTS, D_MODEL)) * 0.1
    return {"x": x, "mix_norm_g": mix_norm_g, "w_in": w_in,
            "ssm_a_re": ssm_a_re, "ssm_a_im": ssm_a_im, "ssm_log_step": ssm_log_step,
            "ssm_b_re": ssm_b_re, "ssm_b_im": ssm_b_im, "ssm_c_re": ssm_c_re, "ssm_c_im": ssm_c_im,
            "ssm_d": ssm_d, "ssm_w_glu": ssm_w_glu, "fox_forget_bias": fox_forget_bias,
            "q_norm_g": q_norm_g, "k_norm_g": k_norm_g, "w_out": w_out, "ffn_norm_g": ffn_norm_g,
            "peer_w_query": peer_w_query, "peer_sub_keys": peer_sub_keys,
            "peer_u": peer_u, "peer_v": peer_v}

def second_block(x, mix_norm_g, w_in, ssm_a_re, ssm_a_im, ssm_log_step, ssm_b_re, ssm_b_im,
              ssm_c_re, ssm_c_im, ssm_d, ssm_w_glu, fox_forget_bias, q_norm_g, k_norm_g,
              w_out, ffn_norm_g, peer_w_query, peer_sub_keys, peer_u, peer_v):
    for layer in range(DEPTH):
        h = rms_norm(x, mix_norm_g[layer])
        proj = h @ w_in[layer]
        u, q, k, v, f_logit, g_ssm, g_att = jnp.split(proj, IN_SPLITS, axis=-1)
        y_ssm = s5_branch(u, ssm_a_re[layer], ssm_a_im[layer], ssm_log_step[layer],
                          ssm_b_re[layer], ssm_b_im[layer], ssm_c_re[layer], ssm_c_im[layer],
                          ssm_d[layer], ssm_w_glu[layer])
        y_att = forgetting_attention(q, k, v, f_logit, fox_forget_bias[layer],
                                     q_norm_g[layer], k_norm_g[layer])
        merged = jax.nn.sigmoid(g_ssm) * y_ssm + jax.nn.sigmoid(g_att) * y_att
        x = x + (merged @ w_out[layer]).astype(x.dtype)
        h2 = rms_norm(x, ffn_norm_g[layer])
        x = x + peer_ffn(h2, peer_w_query[layer], peer_sub_keys[layer],
                         peer_u[layer], peer_v[layer]).astype(x.dtype)
    return x


def setup_inputs(seed=0):
    out = dict(first_inputs(seed))
    for name, value in second_inputs(seed + 1).items():
        if name != "x":
            out[name + "_2"] = value
    return out


def reference(
    x, c, ctx, c_ctx, w_mod, b_mod, g_norm1, w_in, conv_w, conv_b, lru_lam, lru_wa, lru_ba,
    lru_wx, lru_bx, g_v, w_s, b_s, w_pr, w_pg, w_out, g_norm2, w_up, ffn_conv_w, ffn_conv_b,
    w_down, g_final, mix_norm_g_2, w_in_2, ssm_a_re_2, ssm_a_im_2, ssm_log_step_2, ssm_b_re_2,
    ssm_b_im_2, ssm_c_re_2, ssm_c_im_2, ssm_d_2, ssm_w_glu_2, fox_forget_bias_2, q_norm_g_2,
    k_norm_g_2, w_out_2, ffn_norm_g_2, peer_w_query_2, peer_sub_keys_2, peer_u_2, peer_v_2,
):
    x = first_block(
        x, c, ctx, c_ctx, w_mod, b_mod, g_norm1, w_in, conv_w, conv_b, lru_lam, lru_wa, lru_ba,
        lru_wx, lru_bx, g_v, w_s, b_s, w_pr, w_pg, w_out, g_norm2, w_up, ffn_conv_w, ffn_conv_b,
        w_down, g_final,
    )
    return second_block(
        x, mix_norm_g_2, w_in_2, ssm_a_re_2, ssm_a_im_2, ssm_log_step_2, ssm_b_re_2, ssm_b_im_2,
        ssm_c_re_2, ssm_c_im_2, ssm_d_2, ssm_w_glu_2, fox_forget_bias_2, q_norm_g_2, k_norm_g_2,
        w_out_2, ffn_norm_g_2, peer_w_query_2, peer_sub_keys_2, peer_u_2, peer_v_2,
    )


_drawn_inputs = setup_inputs


def setup_inputs(seed=0):
    import zlib

    import numpy as np

    out = dict(_drawn_inputs(seed))
    spreads = {}
    factors = {'mix_norm_g_2': 8.0,
     'ssm_a_re_2': 64.0,
     'ssm_a_im_2': 64.0,
     'ssm_log_step_2': 64.0,
     'ssm_b_re_2': 64.0,
     'ssm_b_im_2': 64.0,
     'ssm_c_re_2': 64.0,
     'ssm_c_im_2': 64.0,
     'fox_forget_bias_2': 4.307,
     'q_norm_g_2': 8.0,
     'k_norm_g_2': 8.0,
     'ffn_norm_g_2': 8.0,
     'peer_w_query_2': 3.311,
     'peer_sub_keys_2': 3.299,
     'peer_u_2': 3.655,
     'peer_v_2': 3.305}
    for name, (base, spread) in spreads.items():
        noise = np.random.default_rng([zlib.crc32(name.encode()), seed]).standard_normal(out[name].shape)
        drawn = base * np.exp(spread * noise) if base else spread * noise
        out[name] = __import__('jax').numpy.asarray(drawn.astype(out[name].dtype))
    for name, factor in factors.items():
        out[name] = (out[name] * factor).astype(out[name].dtype)
    return out
```

```python
import math
from contextlib import ExitStack

import numpy as np

import concourse.bass as bass
from concourse import mybir

F32 = mybir.dt.float32
U32 = mybir.dt.uint32
ACT = mybir.ActivationFunctionType
ALU = mybir.AluOpType
AX = mybir.AxisListType.X

P = 128
T, TC = 512, 256
TX = T + TC
D = 1024
KD = D // P
W_R = 1280
NR = W_R // P
KR = 4
W_G = 1024
HG = 8
D_FF = 2816
NF = D_FF // P
GW = 64
GH = T // GW
EPS = 1e-6
SSM = 512
KS = SSM // P
NS = 16
HEADS = 8
PH, PK, TOPK = 8, 128, 16
NSLOT = PH * TOPK
R = 4
SLOT = 11 * P
NB = T // P
JG = 8
TG = 64
TWO_PI = 2.0 * math.pi
ROUND = 1.5 * 2.0 ** 23
PI_LESS = 3.1415925
NEG = -1e30

VECS = [("c2", 2 * KD), ("bmod", 48), ("g1", KD), ("convw", NR * KR), ("convb", NR), ("lam", 2 * NR),
        ("ba", 2 * NR), ("bx", 2 * NR), ("gv", HG), ("g2", KD), ("fcw", NF * 9), ("fcb", NF), ("gfin", KD),
        ("mixg", KD), ("are", NS), ("aim", NS), ("lstep", NS), ("dskip", KS), ("fbias", 1), ("qg", 1),
        ("kg", 1), ("ffng", KD), ("eps", 1)]
VCOL, _at = {}, 0
for _n, _w in VECS:
    VCOL[_n] = _at
    _at += _w
NVEC = _at

STAGES = [
    ("moda", 16, ["T"], None),
    ("rx", NR, ["B", "BT"], lambda j: ("pad_ready", j + 1)),
    ("gates", 2 * NR, ["B", "B", "B", "BT"], lambda j: ("gate_tanh", j + 1)),
    ("rg", NR, ["BT"], lambda j: ("rg_gelu", j + 1)),
    ("modb", 32, ["T"], None),
    ("v", 8, ["T"], None),
    ("mix", 1, ["B"] * (HG - 1) + ["BT"], lambda j: ("yg_mixed", j + 1)),
    ("u", HG, ["BT"], lambda j: ("u_gelu", j + 1)),
    ("merge", KD, ["BT"] * 4, lambda j: (("merge_tanh", "merge_mul")[j % 2], 2 * (j // 4) + 1 + j % 4 // 2)),
    ("out", KD, ["BT"], lambda j: ("x_mixed", j + 1)),
    ("up", NF, ["BT", "BT"], lambda j: (("ffpad_ready", "ff_ready")[j % 2], j // 2 + 1)),
    ("down", KD, ["T", "BT"], lambda j: ("x_ffn", j + 1)),
    ("u2", KS, ["BT"], lambda j: ("u2_ready", j + 1)),
    ("ssm", NS, ["T"], None),
    ("glu", KD, ["B", "BT", "BT"],
     lambda j: ("glu_mul", j // 3 + 1) if j % 3 == 0 else ("glu_tanh", 2 * (j // 3) + j % 3)),
    ("q", KD, ["BT"], lambda j: ("q_ready", j + 1)),
    ("k", KD, ["BT"], lambda j: ("k_ready", j + 1)),
    ("v2", 8, ["T"], None),
    ("f", 1, ["BT"], lambda j: ("f_read", 1)),
    ("attn", HEADS, ["B"] * (2 * NB + 1),
     lambda j: [("p_exp", NB * (j // 9) + j % 9 + 1), ("pt_ready", NB * (j // 9) + j % 9 - NB + 1),
                ("o_ready", j // 9 + 1)][j % 9 // NB]),
    ("ga", KD, ["BT"], lambda j: ("ga_tanh", j + 1)),
    ("out2", KD, ["BT"], lambda j: ("x_mixed2", j + 1)),
    ("query", 16, ["BT"], lambda j: ("pq_ready", j + 1)),
    ("keys", 2, ["B"] * 7 + ["BT"], lambda j: ("sc_ready", j + 1)),
    ("gate", T // 4, ["B"], lambda j: ("gates_staged", j + 1)),
    ("experts", PK, ["T"], None),
]
TILE0, BLOCK0, USED, DONE, READ = {}, {}, [], [], []
_count = 0
for _name, _units, _signals, _reader in STAGES:
    TILE0[_name], BLOCK0[_name] = len(USED), len(DONE)
    for _k in range(_units * len(_signals)):
        _count += 1
        if "T" in _signals[_k % len(_signals)]:
            USED.append(_count)
        if "B" in _signals[_k % len(_signals)]:
            READ.append(_reader(len(DONE) - BLOCK0[_name]))
            DONE.append(_count)


class At:

    def __init__(self, first, i=0, step=0):
        assert step % R == 0
        self.first, self.i, self.step = first, i, step
        self.slot = first % R
        self.turn = i * (step // R) + first // R
        self.fresh = isinstance(i, int) and first + i * step < R

    def of(self, table, back=0):
        first = self.first - back
        if isinstance(self.i, int):
            return table[first + self.i * self.step]
        one, two = table[first + self.step], table[first + 2 * self.step]
        return self.i * (two - one) + (2 * one - two)


def rounds(eng, n, per, body):
    whole = n // per
    if whole >= 3:
        for u in range(per):
            body(u, 0)
        with eng.Fori(1, whole) as i:
            for u in range(per):
                body(u, i)
    else:
        for i in range(whole):
            for u in range(per):
                body(u, i)
    for u in range(n % per):
        body(u, whole)


def wait(eng, sem, value):
    if not isinstance(value, int) or value > 0:
        eng.wait_ge(sem, value)


def chain(eng, sem, base=0):
    done = [0]

    def link(ins):
        done[0] += 1
        ins.then_inc(sem, 1)
        eng.wait_ge(sem, base + done[0])
        return ins
    return link


def build(nc, io):
    with ExitStack() as ctx:
        sems = {}

        def S(name):
            if name not in sems:
                sems[name] = ctx.enter_context(nc.semaphore(name))
            return sems[name]

        def sb(name, cols, dt=F32):
            return ctx.enter_context(nc.sbuf_tensor(name, [P, cols], dt))

        ring_t = sb("ring", R * SLOT)
        x_t, h_t, y_t = sb("x", KD * T), sb("h", KD * TX), sb("y", NR * T)
        z_t, tmp_t = sb("z", 19456), sb("tmp", 8192)
        vec, mod_t, small = sb("vec", NVEC), sb("mod", 96), sb("small", 1700)
        ones, ident, iota = sb("ones", P), sb("ident", P), sb("iota", P)
        rstd, sd = sb("rstd", TX), sb("sd", TX)
        psum = ctx.enter_context(nc.psum_tensor("psum", [P, 8, T], F32))
        gates_d = nc.dram_tensor("gates_scratch", (P, PK, T), F32, kind="Internal").ap()

        def view(t, at, c, w):
            return t[:, at:at + c * w].rearrange("p (c w) -> p c w", w=w)

        def pick(t, n):
            if isinstance(n, int):
                return t[:, n, :]
            return t[:, bass.ds(n, 1), :].rearrange("p o w -> p (o w)")

        def dram(name, n):
            if isinstance(n, int):
                return io[name][n]
            return io[name][bass.ds(n, 1)].rearrange("o p w -> p (o w)")

        def col(t, n):
            return t[:, n:n + 1] if isinstance(n, int) else t[:, bass.ds(n, 1)]

        def V(name):
            return vec[:, VCOL[name]:VCOL[name] + dict(VECS)[name]]

        taken = [0]

        def sm(w, dt=F32):
            a = small[:, taken[0]:taken[0] + w]
            taken[0] += w
            assert taken[0] <= 1700
            return a

        def t3(a, w):
            return a.rearrange("p (c w) -> p c w", w=w)

        x = view(x_t, 0, KD, T)
        h = view(h_t, 0, KD, TX)
        h2 = view(h_t, 0, KD, T)
        y = view(y_t, 0, NR, T)
        mod = mod_t[:, :].rearrange("p (n k) -> p n k", k=2)
        tmp = view(tmp_t, 0, 16, T)
        tx = view(tmp_t, 0, 8, 1024)
        xr = view(z_t, 0, NR, TX)
        lw, la, lb = (view(z_t, NR * TX + k * 5 * TX, 5, TX) for k in range(3))
        xc = view(z_t, NR * TX, KD, TX)
        vtok = view(z_t, 0, NB, W_G)
        yg = view(z_t, 4096, HG, T)
        mg = view(z_t, 8192, KD, T)
        bsrow = view(z_t, 12288, HG, P)
        ff = view(z_t, 0, NF, T)
        cosT, sinT = view(z_t, 0, NS, T), view(z_t, NS * T, NS, T)
        mg2 = view(z_t, 0, KD, T)
        qT, kT = view(z_t, 4096, HEADS, T), view(z_t, 8192, HEADS, T)
        vt2 = view(z_t, 12288, NB, D)
        maskt = z_t[:, 16384:16384 + P]
        sel = view(z_t, 16512, HEADS, P)
        cumn = z_t[0:HEADS, 17536:17536 + T]
        pq = view(z_t, 0, 16, T)
        gbuf, ew, evt = view(z_t, 0, JG, T), view(z_t, 4096, JG, T), view(z_t, 8192, JG, D)
        stage = [view(z_t, k * PK * TG, PK, TG) for k in range(2)]
        u2, ys = view(y_t, 0, KS, T), view(y_t, KS * T, KS, T)
        eq, prod = y_t[:, 0:2048], y_t[:, 2048:4096]
        hot_a, hot_b = view(y_t, 0, 2, 4 * P), view(y_t, 1024, 2, 4 * P)
        bw, bt = view(h_t, 4096, 2, 2 * P), view(h_t, 4608, 2, 2 * P)
        bt1, bt2 = h_t[:, 5120:5248], h_t[:, 5248:5376]
        picksT = view(h_t, 4096, 3, T)
        pads = [tmp_t[:, k * 780:k * 780 + 774] for k in range(2)]
        ffpads = [tmp_t[:, 6144 + k * 660:6144 + (k + 1) * 660].rearrange("p (r c) -> p r c", c=GW + 2)
                  for k in range(2)]
        ssm_s = view(tmp_t, 4 * T, 4, T)
        probs, probsT = view(tmp_t, 0, NB, T), view(tmp_t, NB * T, NB, T)
        tops = view(tmp_t, 2048, NB, 16 * TOPK)
        topi = view(tmp_t, 3072, NB, 16 * TOPK)
        topf = view(tmp_t, 4096, NB, 16 * TOPK)
        picks = view(tmp_t, 5120, NB, 3 * P)
        scratch = tmp_t[:, 6656:6912]
        cand = tmp_t[:, 6912:7168]
        best = tmp_t[:, 7168:7296]
        posn, posa, posb = (tmp_t[:, 7296 + k * P:7424 + k * P] for k in range(3))
        bexp, fa, fb = (tmp_t[:, 7680 + k * P:7808 + k * P] for k in range(3))
        fl = [t3(y_t[0:HEADS, :], T)[:, k, :] for k in range(8)]
        silu = t3(sm(2 * KD), 2)
        a1, a2 = t3(sm(2 * KD), 2), sm(KD)
        hm2 = sm(KD)
        sp = [sm(2 * NR) for _ in range(6)]
        sp2, sp4n, hba, hbx = (sm(2 * NR) for _ in range(4))
        vss, vsd, vrs = sm(NB), sm(NB), sm(NB)
        sc = [sm(NS) for _ in range(12)]
        s_step, s_mag, s_cos, s_sin = (sm(NS) for _ in range(4))
        cr, ci = sm(NS), sm(NS)
        pw = sm(10 * 2 * NS).rearrange("p (l k s) -> p l k s", k=2, s=NS)
        nmx, rs, rrs = sm(2 * NB), sm(2 * NB), sm(2 * NB)
        dcol, gsum, grec = sm(KS), sm(PH), sm(PH)

        def slot(at, lo, n):
            return ring_t[:, at.slot * SLOT + lo:at.slot * SLOT + lo + n]

        def wchunk(at, k, w=P):
            return slot(at, k * w, w)

        def bank(at, n=T):
            return psum[:, at.slot, 0:n]

        def tile_at(stage, k, i=0, step=0):
            return At(TILE0[stage] + k, i, step)

        def block_at(stage, k, i=0, step=0):
            return At(BLOCK0[stage] + k, i, step)

        def tile_here(eng, at):
            eng.wait_ge(S(f"tile_loaded{at.slot}"), at.turn * 16 + 16)

        def block_free(eng, at):
            if not at.fresh:
                names = [r[0] for r in READ]
                name = names[at.first - R + (at.step if not isinstance(at.i, int) else at.i * at.step)]
                eng.wait_ge(S(name), at.of([r[1] for r in READ], R))

        def block_here(eng, at):
            eng.wait_ge(S("pe_done"), at.of(DONE))

        def tile_used(eng, at):
            eng.wait_ge(S("pe_done"), at.of(USED))

        def skip(ve, oc):
            tile_used(ve, tile_at("ssm", 4 * oc + 3))
            wait(ve, S("ysg_ready"), oc - 1)
            nc.vector.scalar_tensor_tensor(tmp[:, 14 + oc % 2, :], u2[:, oc, :], V("dskip")[:, oc:oc + 1],
                                           psum[:, 7, :], ALU.mult, ALU.add).then_inc(S("ys_read"), 1)

        block = ctx.enter_context(nc.Block())

        @block.sync
        def _(sp):
            def fetch(at, src, n):
                if not at.fresh:
                    sp.wait_ge(S("pe_done"), at.of(USED, R))
                sp.dma_start(slot(at, 0, n), src).then_inc(S(f"tile_loaded{at.slot}"), 16)

            def stream(stage, name, n, size, per=4):
                def body(u, i):
                    fetch(tile_at(stage, u, i, per), dram(name, i * per + u), size)
                rounds(sp, n, per, body)

            sp.dma_start(vec[:, :], io["vecs"]).then_inc(S("vecs_loaded"), 16)
            sp.dma_start(xc, io["xc"]).then_inc(S("x_loaded"), 16)
            stream("moda", "w_moda", 16, KD * P)
            sp.dma_start(x, io["xT"]).then_inc(S("xres_loaded"), 16)
            stream("rx", "w_rx", NR, KD * P)
            stream("gates", "w_gates", 2 * NR, 4 * P)
            stream("rg", "w_rg", NR, KD * P)
            stream("modb", "w_modb", 32, KD * P)
            stream("v", "w_v", 8, 2 * 512)
            fetch(tile_at("mix", 0), io["w_sT"], HG * P)
            sp.wait_ge(S("lru_done"), 2 * NR)
            sp.dma_start(bsrow, io["bsrow"]).then_inc(S("bsrow_loaded"), 16)
            stream("u", "w_u", HG, KD * P)

            def merge(u, i):
                for k, (name, c) in enumerate((("w_gr", KD), ("w_pr", NR), ("w_gg", KD), ("w_pg", KD))):
                    fetch(tile_at("merge", k, i, 4), dram(name, i), c * P)
            rounds(sp, KD, 1, merge)
            stream("out", "w_out", KD, KD * P)
            stream("up", "w_up", 2 * NF, KD * P)
            stream("down", "w_down", 2 * KD, SLOT)
            stream("u2", "w_u2", KS, KD * P)
            stream("ssm", "w_ssm", NS, 4 * P)
            stream("glu", "w_glu", 2 * KD, KD * P)
            stream("q", "w_q", KD, KD * P)
            stream("k", "w_k", KD, KD * P)
            stream("v2", "w_v2", 8, 2 * 512)
            fetch(tile_at("f", 0), io["w_f"], KD * HEADS)
            stream("ga", "w_ga", KD, KD * P)
            stream("out2", "w_out2", KD, KD * P)
            stream("query", "w_query", 16, KD * P)
            stream("keys", "w_keys", 2, 8 * P)

            for k in range(R):
                fetch(tile_at("experts", k), dram("u_tab", k), D)
            for g in range(T // TG):
                sp.wait_ge(S("gates_staged"), (g + 1) * (TG // 4))
                sp.dma_start(gates_d[:, :, g * TG:(g + 1) * TG], stage[g % 2])\
                    .then_inc(S(f"gates_parked{g % 2}"), 16)
            for k in range(2):
                sp.wait_ge(S(f"gates_parked{k}"), 16 * (T // TG // 2))

            def experts(i, first):
                for k in range(first, JG):
                    fetch(tile_at("experts", k, i, JG), dram("u_tab", i * JG + k), D)
                    if k == max(first, 2):
                        wait(sp, S("ew_ready"), i * JG)
                        sp.dma_start(gbuf, gates_of(i)).then_inc(S("gates_back"), 16)
                        wait(sp, S("eo_done"), i * KD)
                        sp.dma_start(evt, vtab_of(i)).then_inc(S("vtab_loaded"), 16)

            gd = gates_d.rearrange("p (g a) t -> g p a t", a=JG)
            vd = io["v_tab"]

            def gates_of(i):
                return gd[i] if isinstance(i, int) else gd[bass.ds(i, 1)].rearrange("o p a t -> p (o a) t")

            def vtab_of(i):
                return vd[i] if isinstance(i, int) else vd[bass.ds(i, 1)].rearrange("o p a t -> p (o a) t")
            experts(0, R)
            with sp.Fori(1, PK // JG) as i:
                experts(i, 0)
            for n in range(KD):
                sp.wait_ge(S("eo_read"), (PK // JG - 1) * KD + n + 1)
                sp.dma_start(io["out"][n * P:(n + 1) * P, :], x[:, n, :]).then_inc(S("stored"), 16)
            sp.wait_ge(S("stored"), 16 * KD)

        @block.tensor
        def _(pe):
            PE = S("pe_done")

            def mm(out, lhsT, rhs, first, last, **kw):
                return nc.tensor.matmul(out, lhsT, rhs, start=first, stop=last, **kw)

            def project(stage, n, per, rhs_of, kc=KD, tiles=1):
                def body(u, i):
                    b = block_at(stage, u, i, per)
                    block_free(pe, b)
                    for t in range(tiles):
                        a = tile_at(stage, u * tiles + t, i, per * tiles)
                        tile_here(pe, a)
                        for k in range(kc):
                            last = mm(bank(b), wchunk(a, k), rhs_of(t * kc + k), t + k == 0,
                                      t == tiles - 1 and k == kc - 1)
                        last.then_inc(PE, 1)
                rounds(pe, n, per, body)

            def norm(k, cols):
                wait(pe, S("sd_done"), k)
                for c in range(KD):
                    pe.wait_ge(S("sq_ready"), k * KD + c + 1)
                    at = 8 * T + 1024 * (c % 2)
                    if cols > T:
                        mm(psum[:, 6, 0:cols - T], ones[:, :], tmp_t[:, at + T:at + cols], c == 0, c == KD - 1)
                    mm(psum[:, 5, :], ones[:, :], tmp_t[:, at:at + T], c == 0, c == KD - 1)\
                        .then_inc(S("sq_used"), 1)

            def modulation(stage, first, n):
                for u in range(n):
                    a = tile_at(stage, u)
                    tile_here(pe, a)
                    for k in range(KD):
                        last = mm(psum[:, 4, 2 * (first + u):2 * (first + u) + 2], wchunk(a, k),
                                  silu[:, k, :], k == 0, k == KD - 1)
                    last.then_inc(PE, 1)

            pe.wait_ge(S("silu_ready"), 1)
            modulation("moda", 0, 16)
            pe.wait_ge(S("consts_ready"), 4)
            norm(0, TX)

            def rx(u, i):
                a = tile_at("rx", u, i, 4)
                b0, b1 = block_at("rx", 2 * u, i, 8), block_at("rx", 2 * u + 1, i, 8)
                tile_here(pe, a)
                block_free(pe, b0)
                block_free(pe, b1)
                for k in range(KD):
                    last0 = mm(bank(b0), wchunk(a, k), h[:, k, 0:T], k == 0, k == KD - 1)
                    last1 = mm(bank(b1, TC), wchunk(a, k), h[:, k, T:TX], k == 0, k == KD - 1)
                last0.then_inc(PE, 1)
                last1.then_inc(PE, 1)
            pe.wait_ge(S("norm_done"), KD)
            rounds(pe, NR, 4, rx)

            pe.wait_ge(S("xr_ready"), NR)
            for n in range(2 * NR):
                a = tile_at("gates", n)
                tile_here(pe, a)
                src = 2 * ((n % NR) // 2)
                for g in range(2):
                    for part, (lo, hi) in enumerate(((0, T), (T, TX))):
                        b = block_at("gates", 4 * n + 2 * g + part)
                        block_free(pe, b)
                        for k in range(2):
                            last = mm(bank(b, hi - lo), wchunk(a, 2 * g + k), xr[:, src + k, lo:hi], k == 0, k == 1)
                        last.then_inc(PE, 1)

            project("rg", NR, 4, lambda k: h[:, k, 0:T])
            pe.wait_ge(S("mod_read"), 1)
            modulation("modb", 16, 32)
            pe.wait_ge(S("mod_read"), 2)

            def token_major(stage, src, read):
                for half in range(2):
                    if half:
                        pe.wait_ge(S(read), NB)
                    for kg in range(4):
                        a = tile_at(stage, 4 * half + kg)
                        tile_here(pe, a)
                        for kk in range(2):
                            k = 2 * kg + kk
                            for tb in range(NB):
                                last = mm(psum[:, 4 + tb, :], src[:, k, tb * P:(tb + 1) * P], wchunk(a, kk, 512),
                                          k == 0, k == KD - 1)
                        last.then_inc(PE, 1)
            token_major("v", h, "v_read")

            pe.wait_ge(S("v_normed"), NB)
            a = tile_at("mix", 0)
            tile_here(pe, a)
            for hd in range(HG):
                b = block_at("mix", hd)
                block_free(pe, b)
                for n in range(NB):
                    last = mm(psum[:, b.slot, n * P:(n + 1) * P], vtok[:, n, hd * P:(hd + 1) * P],
                              wchunk(a, hd), True, True)
                last.then_inc(PE, 1)
            project("u", HG, 4, lambda k: h[:, k, 0:T])

            pe.wait_ge(S("yr_ready"), NR)
            pe.wait_ge(S("yg_ready"), HG)

            def merge(u, i):
                for j, (src, kc) in enumerate(((h, KD), (y, NR), (h, KD), (yg, KD))):
                    a, b = tile_at("merge", 4 * u + j, i, 8), block_at("merge", 4 * u + j, i, 8)
                    tile_here(pe, a)
                    block_free(pe, b)
                    for k in range(kc):
                        last = mm(bank(b), wchunk(a, k), src[:, k, 0:T], k == 0, k == kc - 1)
                    last.then_inc(PE, 1)
            rounds(pe, KD, 2, merge)
            pe.wait_ge(S("merged"), KD)
            project("out", KD, 4, lambda k: mg[:, k, :])
            norm(1, T)
            pe.wait_ge(S("norm_done"), 2 * KD)

            def up(u, i):
                for j in range(2):
                    a, b = tile_at("up", 2 * u + j, i, 4), block_at("up", 2 * u + j, i, 4)
                    tile_here(pe, a)
                    block_free(pe, b)
                    for k in range(KD):
                        last = mm(bank(b), wchunk(a, k), h2[:, k, :], k == 0, k == KD - 1)
                    last.then_inc(PE, 1)
            rounds(pe, NF, 2, up)
            pe.wait_ge(S("ff_ready"), NF)
            project("down", KD, 4, lambda k: ff[:, k, :], kc=11, tiles=2)
            norm(2, T)
            norm(3, T)
            pe.wait_ge(S("norm_done"), 4 * KD)
            project("u2", KS, 4, lambda k: h2[:, k, :])

            pe.wait_ge(S("u2_ready"), KS)

            def states_in(c):
                pe.wait_ge(S("bw_ready"), c + 1)
                wait(pe, S("bt_ready"), c)
                for k in range(2):
                    last = nc.tensor.transpose(psum[:, 4, k * P:(k + 1) * P], bw[:, c % 2, k * P:(k + 1) * P],
                                               ident[:, :])
                last.then_inc(S("bt_done"), 1)
                pe.wait_ge(S("bt_ready"), c + 1)
                wait(pe, S("xs_read"), 4 * c)
                for k in range(2):
                    last = mm(psum[:, 5 + k, :], bt[:, c % 2, k * P:(k + 1) * P], u2[:, c // 4, :], True, True)
                last.then_inc(S("xs_done"), 1)

            def states_out(c):
                pe.wait_ge(S("s_ready"), 2 * (c + 1))
                if c % 4 == 0:
                    wait(pe, S("ys_read"), c // 4)
                a = tile_at("ssm", c)
                mm(psum[:, 7, :], wchunk(a, 2), ssm_s[:, 2 * (c % 2), :], c % 4 == 0, False)
                mm(psum[:, 7, :], wchunk(a, 3), ssm_s[:, 2 * (c % 2) + 1, :], False, c % 4 == 3).then_inc(PE, 1)
            states_in(0)
            for c in range(NS):
                if c + 1 < NS:
                    states_in(c + 1)
                tile_here(pe, tile_at("ssm", c))
                states_out(c)

            pe.wait_ge(S("ysg_ready"), KS)

            def glu(u, i):
                a = tile_at("glu", 2 * u, i, 8)
                tile_here(pe, a)
                for j in range(2):
                    b = block_at("glu", 3 * u + j, i, 12)
                    block_free(pe, b)
                    for k in range(KS):
                        last = mm(bank(b), wchunk(a, 4 * j + k), ys[:, k, :], k == 0, k == KS - 1)
                    last.then_inc(PE, 1)
                a, b = tile_at("glu", 2 * u + 1, i, 8), block_at("glu", 3 * u + 2, i, 12)
                tile_here(pe, a)
                block_free(pe, b)
                for k in range(KD):
                    last = mm(bank(b), wchunk(a, k), h2[:, k, :], k == 0, k == KD - 1)
                last.then_inc(PE, 1)
            rounds(pe, KD, 4, glu)
            project("q", KD, 4, lambda k: h2[:, k, :])
            project("k", KD, 4, lambda k: h2[:, k, :])
            token_major("v2", h2, "v2_read")
            a, b = tile_at("f", 0), block_at("f", 0)
            tile_here(pe, a)
            block_free(pe, b)
            for k in range(KD):
                last = mm(psum[0:HEADS, b.slot, :], wchunk(a, k, HEADS), h2[:, k, :], k == 0, k == KD - 1)
            last.then_inc(PE, 1)

            pe.wait_ge(S("v2_read"), 2 * NB)
            for n in range(2 * HEADS):
                pe.wait_ge(S("hsq_ready"), n + 1)
                wait(pe, S("hsd_done"), n - 1)
                mm(psum[:, 4 + n % 2, :], ones[:, :], tmp[:, n % 2, :], True, True).then_inc(S("hss_done"), 1)

            pe.wait_ge(S("cum_ready"), 1)
            pe.wait_ge(S("mask_ready"), 2)
            for hd in range(HEADS):
                pe.wait_ge(S("qk_normed"), HEADS + hd + 1)
                for qb in range(NB):
                    b = block_at("attn", 9 * hd + qb)
                    block_free(pe, b)
                    nk = (qb + 1) * P
                    out = bank(b, nk)
                    mm(out, qT[:, hd, qb * P:(qb + 1) * P], kT[:, hd, 0:nk], True, False)
                    mm(out, sel[0:HEADS, hd, :], cumn[:, 0:nk], False, False)
                    mm(psum[:, b.slot, qb * P:nk], ident[:, :], maskt, False, True).then_inc(PE, 1)
                pe.wait_ge(S("p_ready"), NB * (hd + 1))
                for kb in range(NB):
                    b = block_at("attn", 9 * hd + NB + kb)
                    block_free(pe, b)
                    for qb in range(kb, NB):
                        last = nc.tensor.transpose(psum[:, b.slot, qb * P:(qb + 1) * P],
                                                   probs[:, qb, kb * P:(kb + 1) * P], ident[:, :])
                    last.then_inc(PE, 1)
                b = block_at("attn", 9 * hd + 2 * NB)
                block_free(pe, b)
                for kb in range(NB):
                    pe.wait_ge(S("pt_ready"), NB * hd + kb + 1)
                    last = mm(psum[:, b.slot, kb * P:T], vt2[:, kb, hd * P:(hd + 1) * P],
                              probsT[:, kb, kb * P:T], kb == 0, kb == NB - 1)
                last.then_inc(PE, 1)
            project("ga", KD, 4, lambda k: h2[:, k, :])
            pe.wait_ge(S("merged2"), KD)
            project("out2", KD, 4, lambda k: mg2[:, k, :])
            norm(4, T)
            pe.wait_ge(S("norm_done"), 5 * KD)
            project("query", 16, 4, lambda k: h2[:, k, :])
            pe.wait_ge(S("pq_ready"), 16)
            for n in range(16):
                a, b = tile_at("keys", n // 8), block_at("keys", n)
                tile_here(pe, a)
                block_free(pe, b)
                for tb in range(NB):
                    last = mm(psum[:, b.slot, tb * P:(tb + 1) * P], pq[:, n, tb * P:(tb + 1) * P],
                              wchunk(a, n % 8), True, True)
                last.then_inc(PE, 1)

            for tb in range(NB):
                pe.wait_ge(S("picks_ready"), tb + 1)
                wait(pe, S("picksT_ready"), tb)
                for k in range(3):
                    last = nc.tensor.transpose(psum[:, 4, k * P:(k + 1) * P], picks[:, tb, k * P:(k + 1) * P],
                                               ident[:, :])
                last.then_inc(S("picksT_done"), 1)

            def spread(u, i):
                b = block_at("gate", u, i, 4)
                block_free(pe, b)
                pe.wait_ge(S("hot_ready"), i * 4 + u + 1)
                for k in range(4):
                    last = mm(psum[:, b.slot, k * P:(k + 1) * P], hot_a[:, u % 2, k * P:(k + 1) * P],
                              hot_b[:, u % 2, k * P:(k + 1) * P], True, True)
                last.then_inc(PE, 1)
            rounds(pe, T // 4, 4, spread)

            pe.wait_ge(S("gates_staged"), T // 4)

            def group(i):
                for k in range(JG):
                    a = tile_at("experts", k, i, JG)
                    tile_here(pe, a)
                    wait(pe, S("ea_ready"), i * JG + (k - 3))
                    for c in range(KD):
                        last = mm(psum[:, k % 4, :], wchunk(a, c), h2[:, c, :], c == 0, c == KD - 1)
                    last.then_inc(PE, 1)
                pe.wait_ge(S("ew_ready"), i * JG + JG)
                pe.wait_ge(S("vtab_loaded"), i * 16 + 16)
                for dc in range(KD):
                    wait(pe, S("eo_read"), i * KD + (dc - 3))
                    for k in range(JG):
                        last = mm(psum[:, 4 + dc % 4, :], evt[:, k, dc * P:(dc + 1) * P], ew[:, k, :],
                                  k == 0, k == JG - 1)
                    last.then_inc(S("eo_done"), 1)
            group(0)
            with pe.Fori(1, PK // JG) as i:
                group(i)

        @block.scalar
        def _(act):
            A = nc.scalar.activation

            act.wait_ge(S("vecs_loaded"), 16)
            A(silu, t3(V("c2"), 2), ACT.Silu).then_inc(S("silu_ready"), 1)
            act.wait_ge(S("sp_abs"), 1)
            A(sp[1], sp[0], ACT.Exp, scale=-1.0).then_inc(S("sp_exp"), 1)
            act.wait_ge(S("sp_one"), 1)
            A(sp[3], sp[2], ACT.Ln).then_inc(S("sp_ln"), 1)

            def norm(k, src, cols, ready, first):
                for c in range(KD):
                    act.wait_ge(S(ready), first(c))
                    wait(act, S("sq_used"), k * KD + c - 1)
                    at = 8 * T + 1024 * (c % 2)
                    A(tmp_t[:, at:at + cols], src[:, c, 0:cols], ACT.Square).then_inc(S("sq_ready"), 1)
                act.wait_ge(S("sq_used"), (k + 1) * KD)
                wait(act, S("norm_done"), k * KD)
                if cols > T:
                    A(sd[:, T:cols], psum[:, 6, 0:cols - T], ACT.Sqrt, scale=1.0 / D, bias=epsc)
                A(sd[:, 0:T], psum[:, 5, :], ACT.Sqrt, scale=1.0 / D, bias=epsc).then_inc(S("sd_done"), 1)
            epsc = ones[:, 0:1] if False else V("eps")
            norm(0, xc, TX, "x_loaded", lambda c: 16)

            def rx(u, i):
                n = i * 4 + u
                b0, b1 = block_at("rx", 2 * u, i, 8), block_at("rx", 2 * u + 1, i, 8)
                pad = pads[u % 2]
                wait(act, S("xr_ready"), n - 1)
                block_here(act, b0)
                A(pad[:, 2:2 + T], bank(b0), ACT.Copy).then_inc(S("pad_ready"), 1)
                block_here(act, b1)
                A(pad[:, T + 5:T + 5 + TC], bank(b1, TC), ACT.Copy).then_inc(S("pad_ready"), 1)
            act.wait_ge(S("pads_zero"), 2)
            rounds(act, NR, 4, rx)

            act.wait_ge(S("sp_done"), 1)
            act.wait_ge(S("xr_ready"), NR)
            for n in range(2 * NR):
                j = n % 5
                rr, ri = tx[:, 2 * (n % 2), 0:TX], tx[:, 2 * (n % 2) + 1, 0:TX]
                wait(act, S("lru_in"), n - 1)
                for g, (dst, bias) in enumerate(((rr, hba), (ri, hbx))):
                    for part, (lo, hi) in enumerate(((0, T), (T, TX))):
                        b = block_at("gates", 4 * n + 2 * g + part)
                        block_here(act, b)
                        A(dst[:, lo:hi], bank(b, hi - lo), ACT.Tanh, scale=0.5, bias=bias[:, n:n + 1])\
                            .then_inc(S("gate_tanh"), 1)
                wait(act, S("lru_done"), 5 * (n // 5))
                act.wait_ge(S("gate_tanh"), 4 * n + 2)
                A(lw[:, j, :], rr, ACT.Tanh, scale=sp2[:, n:n + 1], bias=sp2[:, n:n + 1]).then_inc(S("decay"), 1)
                A(la[:, j, :], rr, ACT.Exp, scale=sp4n[:, n:n + 1], bias=sp4n[:, n:n + 1]).then_inc(S("decay"), 1)
                if j == 4:
                    for k in range(5):
                        act.wait_ge(S("a_ready"), n - 4 + k + 1)
                        A(lw[:, k, :], lw[:, k, :], ACT.Sqrt).then_inc(S("root"), 1)

            act.wait_ge(S("lru_done"), 2 * NR)

            def gelu_into(stage, sem, used, base):
                def body(u, i):
                    n = i * 4 + u
                    b = block_at(stage, u, i, 4)
                    block_here(act, b)
                    wait(act, S(used), n - 1)
                    A(tmp[:, u % 2, :], bank(b), ACT.Gelu_apprx_tanh).then_inc(S(sem), 1)
                return body
            rounds(act, NR, 4, gelu_into("rg", "rg_gelu", "yr_ready", 0))

            for half in range(2):
                tile_used(act, tile_at("v", 4 * half + 3))
                for tb in range(NB):
                    A(vtok[:, tb, half * 512:(half + 1) * 512], psum[:, 4 + tb, :], ACT.Gelu_apprx_tanh)\
                        .then_inc(S("v_read"), 1)
            act.wait_ge(S("v_read"), 2 * NB)
            for tb in range(NB):
                if tb:
                    act.wait_ge(S("v_sq"), tb)
                A(tmp_t[:, 4 * T:4 * T + W_G], vtok[:, tb, :], ACT.Square, accum_out=vss[:, tb:tb + 1])\
                    .then_inc(S("v_sq"), 1)
            act.wait_ge(S("v_sq"), NB)
            A(vsd, vss, ACT.Sqrt, scale=1.0 / W_G, bias=epsc).then_inc(S("v_sd"), 1)
            act.wait_ge(S("yr_ready"), NR)
            rounds(act, HG, 4, gelu_into("u", "u_gelu", "yg_ready", 0))
            act.wait_ge(S("yg_ready"), HG)

            def merge(u, i):
                for j in range(2):
                    b = block_at("merge", 4 * u + 2 * j, i, 8)
                    block_here(act, b)
                    wait(act, S("merge_mul"), 2 * (i * 2 + u) + (j + 1 - 4))
                    A(tmp[:, 2 * (u % 2) + j, :], bank(b), ACT.Tanh, scale=0.5).then_inc(S("merge_tanh"), 1)
            rounds(act, KD, 2, merge)
            norm(1, x, T, "x_mixed", lambda c: c + 1)

            act.wait_ge(S("ffpads_zero"), 2)

            def up(u, i):
                if u:
                    return
                for u in range(2):
                    b = block_at("up", 2 * u, i, 4)
                    wait(act, S("ffconv"), 9 * (i * 2 + (u - 1)))
                    block_here(act, b)
                    A(ffpads[u][:, 1:1 + GH, 1:1 + GW], bank(b).rearrange("p (r c) -> p r c", c=GW), ACT.Copy)\
                        .then_inc(S("ffpad_ready"), 1)
                for u in range(2):
                    act.wait_ge(S("ffconv"), 9 * (i * 2 + (u + 1)))
                    wait(act, S("ff_ready"), i * 2 + (u - 1))
                    A(tmp[:, 2 + u, :], tmp[:, u, :], ACT.Gelu_apprx_tanh).then_inc(S("ff_gelu"), 1)
            rounds(act, NF, 2, up)
            norm(2, x, T, "x_ffn", lambda c: c + 1)
            norm(3, x, T, "norm_done", lambda c: 2 * KD + c + 1)

            def copy_out(stage, dst, sem, per=4):
                def body(u, i):
                    b = block_at(stage, u, i, per)
                    block_here(act, b)
                    A(pick(dst, i * per + u), bank(b), ACT.Copy).then_inc(S(sem), 1)
                return body
            rounds(act, KS, 4, copy_out("u2", u2, "u2_ready"))

            A(s_step, V("lstep"), ACT.Exp).then_inc(S("s5_act"), 1)
            act.wait_ge(S("s5_dve"), 1)
            A(s_mag, sc[0], ACT.Exp).then_inc(S("s5_act"), 1)
            act.wait_ge(S("s5_dve"), 2)
            A(s_sin, sc[1], ACT.Sin).then_inc(S("s5_act"), 1)
            A(s_cos, sc[2], ACT.Sin).then_inc(S("s5_act"), 1)
            for c in range(NS):
                act.wait_ge(S("bt_done"), c + 1)
                wait(act, S("xs_done"), c - 1)
                A(bt[:, c % 2, :], psum[:, 4, 0:2 * P], ACT.Copy).then_inc(S("bt_ready"), 1)
                if c % 4 == 3 and c > 3:
                    act.wait_ge(S("ys_read"), c // 4)
                    A(ys[:, c // 4 - 1, :], tmp[:, 14 + (c // 4 - 1) % 2, :], ACT.Gelu_apprx_tanh)\
                        .then_inc(S("ysg_ready"), 1)
            act.wait_ge(S("ys_read"), KS)
            A(ys[:, KS - 1, :], tmp[:, 14 + (KS - 1) % 2, :], ACT.Gelu_apprx_tanh).then_inc(S("ysg_ready"), 1)

            def glu(u, i):
                for j in range(2):
                    b = block_at("glu", 3 * u + 1 + j, i, 12)
                    block_here(act, b)
                    wait(act, S("glu_done"), i * 4 + (u - 1))
                    A(tmp[:, 2 * (u % 2) + j, :], bank(b), ACT.Tanh, scale=0.5).then_inc(S("glu_tanh"), 1)
            rounds(act, KD, 4, glu)
            rounds(act, KD, 4, copy_out("q", qT, "q_ready"))
            rounds(act, KD, 4, copy_out("k", kT, "k_ready"))
            for half in range(2):
                tile_used(act, tile_at("v2", 4 * half + 3))
                for tb in range(NB):
                    A(vt2[:, tb, half * 512:(half + 1) * 512], psum[:, 4 + tb, :], ACT.Copy).then_inc(S("v2_read"), 1)
            act.wait_ge(S("f_abs"), 1)
            A(fl[1], fl[2], ACT.Exp, scale=-1.0).then_inc(S("f_act"), 1)
            act.wait_ge(S("f_one"), 1)
            A(fl[4], fl[3], ACT.Ln).then_inc(S("f_act"), 1)

            act.wait_ge(S("glu_done"), KD)
            act.wait_ge(S("q_ready"), KD)
            act.wait_ge(S("k_ready"), KD)

            def head_square(n):
                wait(act, S("hss_done"), n - 1)
                src = (qT if n < HEADS else kT)[:, n % HEADS, :]
                A(tmp[:, n % 2, :], src, ACT.Square).then_inc(S("hsq_ready"), 1)
            head_square(0)
            for n in range(2 * HEADS):
                if n + 1 < 2 * HEADS:
                    head_square(n + 1)
                act.wait_ge(S("hss_done"), n + 1)
                wait(act, S("qk_normed"), n - 1)
                A(tmp[:, 2 + n % 2, :], psum[:, 4 + n % 2, :], ACT.Sqrt, scale=1.0 / P, bias=epsc)\
                    .then_inc(S("hsd_done"), 1)

            act.wait_ge(S("qk_normed"), 2 * HEADS)
            for hd in range(HEADS):
                for qb in range(NB):
                    at = NB * (hd % 2) + qb
                    act.wait_ge(S("amax"), NB * hd + qb + 1)
                    if hd:
                        block_here(act, block_at("attn", 9 * (hd - 1) + 2 * NB - 1))
                    A(probs[:, qb, 0:(qb + 1) * P], bank(block_at("attn", 9 * hd + qb), (qb + 1) * P), ACT.Exp,
                      bias=nmx[:, at:at + 1], accum_out=rs[:, at:at + 1]).then_inc(S("p_exp"), 1)
                b = block_at("attn", 9 * hd + 2 * NB)
                block_here(act, b)
                A(y[:, hd, :], bank(b), ACT.Copy).then_inc(S("o_ready"), 1)

            def ga(u, i):
                b = block_at("ga", u, i, 4)
                block_here(act, b)
                wait(act, S("merged2"), i * 4 + (u - 1))
                A(tmp[:, 8 + u % 2, :], bank(b), ACT.Tanh, scale=0.5).then_inc(S("ga_tanh"), 1)
            rounds(act, KD, 4, ga)
            norm(4, x, T, "x_mixed2", lambda c: c + 1)
            rounds(act, 16, 4, copy_out("query", pq, "pq_ready"))
            for n in range(16):
                b = block_at("keys", n)
                block_here(act, b)
                wait(act, S("topk_done"), n - 3)
                A(tmp[:, n % 4, :], bank(b), ACT.Copy).then_inc(S("sc_ready"), 1)
            for tb in range(NB):
                act.wait_ge(S("best_ready"), tb + 1)
                A(bexp, fa, ACT.Exp).then_inc(S("best_exp"), 1)
                act.wait_ge(S("picksT_done"), tb + 1)
                A(picksT[:, :, tb * P:(tb + 1) * P], t3(psum[:, 4, 0:3 * P], P), ACT.Copy)\
                    .then_inc(S("picksT_ready"), 1)

            def spread(u, i):
                n = i * 32 + u
                if u % 16 == 0:
                    wait(act, S(f"gates_parked{u // 16}"), i * 16)
                b = block_at("gate", u, i, 32)
                block_here(act, b)
                t0 = 4 * (u % 16)
                A(stage[u // 16][:, :, t0:t0 + 4].rearrange("p j t -> p t j"), t3(bank(b), P), ACT.Copy)\
                    .then_inc(S("gates_staged"), 1)
            act.wait_ge(S("picksT_ready"), NB)
            rounds(act, T // 4, 32, spread)

            def group(i):
                for k in range(JG):
                    tile_used(act, tile_at("experts", k, i, JG))
                    wait(act, S("ew_ready"), i * JG + (k - 3))
                    A(tmp[:, k % 4, :], psum[:, k % 4, :], ACT.Gelu_apprx_tanh).then_inc(S("ea_ready"), 1)
            group(0)
            with act.Fori(1, PK // JG) as i:
                group(i)

        @block.vector
        def _(ve):
            v = nc.vector
            link = chain(ve, S("dve_step"))
            TT, TS, STT = v.tensor_tensor, v.tensor_scalar, v.scalar_tensor_tensor

            for k in range(2):
                v.memset(pads[k], 0.0).then_inc(S("pads_zero"), 1)
            ve.wait_ge(S("vecs_loaded"), 16)

            def log1p_exp(absx, e, one, ln, d, w):
                link(TS(d, one, -1.0, None, ALU.add))
                link(TS(w, d, 2.0 ** -40, None, ALU.max))
                link(v.reciprocal(w, w))
                link(TT(w, w, ln, ALU.mult))
                link(TT(w, w, e, ALU.mult))
                link(STT(d, d, 0.0, e, ALU.is_equal, ALU.mult))
                link(TT(w, w, d, ALU.add))

            link(STT(sp[0], V("lam"), -1.0, V("lam"), ALU.mult, ALU.max))
            ve.sem_inc(S("sp_abs"), 1)
            ve.wait_ge(S("sp_exp"), 1)
            link(TS(sp[2], sp[1], 1.0, None, ALU.add))
            ve.sem_inc(S("sp_one"), 1)
            ve.wait_ge(S("sp_ln"), 1)
            log1p_exp(sp[0], sp[1], sp[2], sp[3], sp[4], sp[5])
            link(TS(sp[4], V("lam"), -1.0, 0.0, ALU.mult, ALU.max))
            link(TT(sp[5], sp[5], sp[4], ALU.add))
            link(TS(sp2, sp[5], 2.0, None, ALU.mult))
            link(TS(sp4n, sp[5], -4.0, None, ALU.mult))
            link(TS(hba, V("ba"), 0.5, None, ALU.mult))
            link(TS(hbx, V("bx"), 0.5, None, ALU.mult))
            ve.sem_inc(S("sp_done"), 1)

            bm = V("bmod").unsqueeze(2).to_broadcast([P, 48, 2])
            pm = psum[:, 4, 0:96].rearrange("p (n k) -> p n k", k=2)
            tile_used(ve, tile_at("moda", 15))
            TT(mod[:, 0:16, :], pm[:, 0:16, :], bm[:, 0:16, :], ALU.add).then_inc(S("mod_read"), 1)
            ve.wait_ge(S("mod_read"), 1)
            for k in range(2):
                link(STT(a1[:, :, k], mod[:, 8:16, k], 1.0, V("g1"), ALU.add, ALU.mult))

            def norm(k, src, dst, cols, scale, shift):
                ve.wait_ge(S("sd_done"), k + 1)
                link(v.reciprocal(rstd[:, 0:cols], sd[:, 0:cols]))
                for c in range(KD):
                    link(TT(dst[:, c, 0:cols], src[:, c, 0:cols], rstd[:, 0:cols], ALU.mult))
                    for j, (lo, hi) in enumerate(((T, cols), (0, T)) if cols > T else ((0, T),)):
                        if cols > T:
                            kk = 1 - j
                            last = TS(dst[:, c, lo:hi], dst[:, c, lo:hi], scale[:, c, kk:kk + 1],
                                      shift[:, c, kk:kk + 1], ALU.mult, ALU.add)
                        elif shift is None:
                            last = TS(dst[:, c, 0:T], dst[:, c, 0:T], scale[:, c:c + 1], None, ALU.mult)
                        else:
                            last = TS(dst[:, c, 0:T], dst[:, c, 0:T], scale[:, c:c + 1], shift[:, c, 0:1],
                                      ALU.mult, ALU.add)
                    last.then_inc(S("norm_done"), 1)
            norm(0, xc, h, TX, a1, mod[:, 0:8, :])

            def rx(u, i):
                n = i * 4 + u
                pad = pads[u % 2]
                step = chain(ve, S("conv_step"), n * 7)
                ve.wait_ge(S("pad_ready"), n * 2 + 2)
                for j, (at, lo, w) in enumerate(((0, 0, T), (T + 3, T, TC))):
                    out = pick(xr, n)[:, lo:lo + w]
                    step(TS(out, pad[:, at:at + w], tap(n, 0), col(V("convb"), n), ALU.mult, ALU.add))
                    for k in range(1, KR):
                        ins = STT(out, pad[:, at + k:at + k + w], tap(n, k), out, ALU.mult, ALU.add)
                        if j == 1 and k == KR - 1:
                            ins.then_inc(S("xr_ready"), 1)
                        else:
                            step(ins)

            def tap(n, k):
                return col(V("convw"), n * KR + k)
            ve.wait_ge(S("pads_zero"), 2)
            rounds(ve, NR, 4, rx)

            def scan_group(g):
                for j in range(5):
                    n = 5 * g + j
                    c = n % NR
                    ri = tx[:, 2 * (n % 2) + 1, 0:TX]
                    ve.wait_ge(S("decay"), 2 * n + 2)
                    link(STT(tx[:, 4, 0:TX], la[:, j, :], 1.0, lw[:, j, :], ALU.add, ALU.mult))
                    TS(la[:, j, :], tx[:, 4, 0:TX], -1.0, 1.0, ALU.mult, ALU.add).then_inc(S("a_ready"), 1)
                    ve.wait_ge(S("gate_tanh"), 4 * n + 4)
                    STT(lb[:, j, :], ri, 1.0, xr[:, c, :], ALU.add, ALU.mult).then_inc(S("lru_in"), 1)
                    ve.wait_ge(S("lru_in"), n + 1)
                    link(STT(lb[:, j, :], la[:, j, :], 1.0, lb[:, j, :], ALU.add, ALU.mult))
                for j in range(5):
                    n = 5 * g + j
                    c = n % NR
                    ve.wait_ge(S("root"), n + 1)
                    link(STT(lb[:, j, :], lb[:, j, :], 0.5, lw[:, j, :], ALU.mult, ALU.mult))
                    aj, bj, cs = la[:, j, :], lb[:, j, :], tx[:, 5, 0:TC]
                    if n < NR:
                        link(v.tensor_tensor_scan(cs, aj[:, T:TX], bj[:, T:TX], 0.0, ALU.mult, ALU.add))
                        v.tensor_tensor_scan(y[:, c, :], aj[:, 0:T], bj[:, 0:T], cs[:, TC - 1:TC], ALU.mult,
                                             ALU.add).then_inc(S("lru_done"), 1)
                    else:
                        link(v.tensor_tensor_scan(cs[:, ::-1], aj[:, T:TX][:, ::-1], bj[:, T:TX][:, ::-1], 0.0,
                                                  ALU.mult, ALU.add))
                        yb = tx[:, 6, 0:T]
                        link(v.tensor_tensor_scan(yb[:, ::-1], aj[:, 0:T][:, ::-1], bj[:, 0:T][:, ::-1],
                                                  cs[:, 0:1], ALU.mult, ALU.add))
                        TT(y[:, c, :], y[:, c, :], yb, ALU.add).then_inc(S("lru_done"), 1)
            ve.wait_ge(S("norm_done"), KD)
            ve.wait_ge(S("xr_ready"), NR)
            for g in range(4):
                scan_group(g)
            ve.wait_ge(S("lru_done"), 2 * NR)

            def times_gelu(dst, sem, ready):
                def body(u, i):
                    n = i * 4 + u
                    ve.wait_ge(S(sem), n + 1)
                    TT(pick(dst, n), pick(dst, n), tmp[:, u % 2, :], ALU.mult).then_inc(S(ready), 1)
                return body
            rounds(ve, NR, 4, times_gelu(y, "rg_gelu", "yr_ready"))

            tile_used(ve, tile_at("modb", 31))
            TT(mod[:, 16:48, :], pm[:, 16:48, :], bm[:, 16:48, :], ALU.add).then_inc(S("mod_read"), 1)
            ve.wait_ge(S("mod_read"), 2)
            link(TS(hm2, mod[:, 16:24, 0], 0.5, None, ALU.mult))
            link(STT(a2, mod[:, 32:40, 0], 1.0, V("g2"), ALU.add, ALU.mult))

            ve.wait_ge(S("v_sd"), 1)
            link(v.reciprocal(vrs, vsd))
            for tb in range(NB):
                TS(vtok[:, tb, :], vtok[:, tb, :], vrs[:, tb:tb + 1], None, ALU.mult).then_inc(S("v_normed"), 1)
            ve.wait_ge(S("bsrow_loaded"), 16)
            for hd in range(HG):
                b = block_at("mix", hd)
                block_here(ve, b)
                STT(t3(yg[:, hd, :], P), t3(bank(b), P), V("gv")[:, hd:hd + 1],
                    bsrow[:, hd:hd + 1, :].to_broadcast([P, NB, P]), ALU.mult, ALU.add)\
                    .then_inc(S("yg_mixed"), 1)
            ve.wait_ge(S("yg_mixed"), HG)
            rounds(ve, HG, 4, times_gelu(yg, "u_gelu", "yg_ready"))

            def merge(u, i):
                n = i * 2 + u
                wait(ve, S("merged"), n - 1)
                for j in range(2):
                    b = block_at("merge", 4 * u + 2 * j + 1, i, 8)
                    block_here(ve, b)
                    ve.wait_ge(S("merge_tanh"), n * 2 + (j + 1))
                    STT(tmp[:, 4 + 2 * (u % 2) + j, :], tmp[:, 2 * (u % 2) + j, :], 1.0, bank(b), ALU.add, ALU.mult)\
                        .then_inc(S("merge_mul"), 1)
                ve.wait_ge(S("merge_mul"), n * 2 + 2)
                TT(pick(mg, n), tmp[:, 4 + 2 * (u % 2), :], tmp[:, 5 + 2 * (u % 2), :], ALU.add).then_inc(S("merged"), 1)
            rounds(ve, KD, 2, merge)

            def add_to_x(stage, sem, scale):
                def body(u, i):
                    n = i * 4 + u
                    b = block_at(stage, u, i, 4)
                    block_here(ve, b)
                    STT(pick(x, n), bank(b), scale(n), pick(x, n), ALU.mult, ALU.add).then_inc(S(sem), 1)
                return body
            ve.wait_ge(S("merged"), KD)
            for k in range(2):
                v.memset(tmp_t[:, 6144 + k * 660:6144 + (k + 1) * 660], 0.0).then_inc(S("ffpads_zero"), 1)
            ve.wait_ge(S("xres_loaded"), 16)
            rounds(ve, KD, 4, add_to_x("out", "x_mixed", lambda n: col(hm2, n)))
            ve.wait_ge(S("x_mixed"), KD)
            norm(1, x, h2, T, a2, mod[:, 24:32, :])

            def up(u, i):
                if u:
                    return
                for u in range(2):
                    n = i * 2 + u
                    cv = tmp[:, u, :].rearrange("p (r c) -> p r c", c=GW)
                    step = chain(ve, S("ffconv"), n * 9)
                    ve.wait_ge(S("ffpad_ready"), n + 1)
                    wait(ve, S("ff_gelu"), n - 1)
                    for t in range(9):
                        win = ffpads[u][:, t // 3:t // 3 + GH, t % 3:t % 3 + GW]
                        w = col(V("fcw"), n * 9 + t)
                        if t == 0:
                            step(TS(cv, win, w, col(V("fcb"), n), ALU.mult, ALU.add))
                        else:
                            step(STT(cv, win, w, cv, ALU.mult, ALU.add))
                for u in range(2):
                    n = i * 2 + u
                    b = block_at("up", 2 * u + 1, i, 4)
                    block_here(ve, b)
                    ve.wait_ge(S("ff_gelu"), n + 1)
                    TT(pick(ff, n), tmp[:, 2 + u, :], bank(b), ALU.mult).then_inc(S("ff_ready"), 1)
            ve.wait_ge(S("ffpads_zero"), 2)
            rounds(ve, NF, 2, up)
            rounds(ve, KD, 4, add_to_x("down", "x_ffn", lambda n: mod_t[:, 80:96:2][:, n:n + 1]
                                       if isinstance(n, int) else mod_t[:, bass.ds(n * 2 + 80, 1)]))
            ve.wait_ge(S("x_ffn"), KD)
            norm(2, x, x, T, V("gfin"), None)
            ve.wait_ge(S("norm_done"), 3 * KD)
            norm(3, x, h2, T, V("mixg"), None)

            ar, ai = V("are"), V("aim")
            ve.wait_ge(S("s5_act"), 1)
            link(TT(sc[0], ar, s_step, ALU.mult))
            link(TT(sc[3], ai, s_step, ALU.mult))
            ve.sem_inc(S("s5_dve"), 1)
            link(TS(sc[4], sc[3], 1.0 / TWO_PI, ROUND, ALU.mult, ALU.add))
            link(TS(sc[4], sc[4], -ROUND, None, ALU.add))
            for part in TWO_PI_PARTS:
                link(STT(sc[3], sc[4], -part, sc[3], ALU.mult, ALU.add))
            link(TS(sc[1], sc[3], PI_LESS, -PI_LESS, ALU.min, ALU.max))
            link(STT(sc[2], sc[1], -1.0, sc[1], ALU.mult, ALU.max))
            link(TS(sc[2], sc[2], -1.0, math.pi / 2, ALU.mult, ALU.add))
            ve.sem_inc(S("s5_dve"), 1)
            ve.wait_ge(S("s5_act"), 4)
            link(TT(sc[5], s_mag, s_cos, ALU.mult))
            link(TS(sc[5], sc[5], -1.0, None, ALU.add))
            link(TT(sc[6], s_mag, s_sin, ALU.mult))
            link(TT(sc[7], ar, ar, ALU.mult))
            link(TT(sc[8], ai, ai, ALU.mult))
            link(TT(sc[7], sc[7], sc[8], ALU.add))
            link(v.reciprocal(sc[7], sc[7]))
            for out, (p, q, op) in ((cr, (sc[5], sc[6], ALU.add)), (ci, (sc[6], sc[5], ALU.subtract))):
                link(TT(sc[8], p, ar, ALU.mult))
                link(TT(sc[9], q, ai, ALU.mult))
                link(TT(sc[8], sc[8], sc[9], op))
                link(TT(out, sc[8], sc[7], ALU.mult))
            link(v.tensor_copy(pw[:, 0, 0, :], s_cos))
            link(v.tensor_copy(pw[:, 0, 1, :], s_sin))
            for k in range(8):
                c0, s0 = pw[:, k, 0, :], pw[:, k, 1, :]
                link(TT(sc[8], c0, c0, ALU.mult))
                link(TT(sc[9], s0, s0, ALU.mult))
                link(TT(pw[:, k + 1, 0, :], sc[8], sc[9], ALU.subtract))
                link(STT(pw[:, k + 1, 1, :], c0, 2.0, s0, ALU.mult, ALU.mult))
            link(v.memset(cosT[:, :, 0:1], 1.0))
            link(v.memset(sinT[:, :, 0:1], 0.0))
            for k in range(9):
                n = 2 ** k
                pc, ps = (pw[:, k, j, :].unsqueeze(2).to_broadcast([P, NS, n]) for j in range(2))
                c0, s0, c1, s1 = cosT[:, :, 0:n], sinT[:, :, 0:n], cosT[:, :, n:2 * n], sinT[:, :, n:2 * n]
                w = tmp_t[:, 0:NS * n].rearrange("p (c w) -> p c w", w=n)
                link(TT(c1, c0, pc, ALU.mult))
                link(TT(w, s0, ps, ALU.mult))
                link(TT(c1, c1, w, ALU.subtract))
                link(TT(s1, s0, pc, ALU.mult))
                link(TT(w, c0, ps, ALU.mult))
                link(TT(s1, s1, w, ALU.add))

            def input_map(c):
                a = tile_at("ssm", c)
                tile_here(ve, a)
                bre, bim = wchunk(a, 0), wchunk(a, 1)
                wait(ve, S("bt_done"), c - 1)
                link(TS(bt1, bim, ci[:, c:c + 1], None, ALU.mult))
                link(STT(bw[:, c % 2, 0:P], bre, cr[:, c:c + 1], bt1, ALU.mult, ALU.subtract))
                link(TS(bt2, bre, ci[:, c:c + 1], None, ALU.mult))
                STT(bw[:, c % 2, P:2 * P], bim, cr[:, c:c + 1], bt2, ALU.mult, ALU.add).then_inc(S("bw_ready"), 1)

            input_map(0)
            for c in range(NS):
                if c + 1 < NS:
                    input_map(c + 1)
                cc, ss = cosT[:, c, :], sinT[:, c, :]
                ve.wait_ge(S("xs_done"), c + 1)
                for k, (bk, tab) in enumerate(((5, cc), (6, ss), (6, cc), (5, ss))):
                    TT(tmp[:, k, :], psum[:, bk, :], tab, ALU.mult).then_inc(S("xs_read"), 1)
                ve.wait_ge(S("xs_read"), 4 * c + 4)
                link(TT(tmp[:, 0, :], tmp[:, 0, :], tmp[:, 1, :], ALU.add))
                link(TT(tmp[:, 2, :], tmp[:, 2, :], tmp[:, 3, :], ALU.subtract))
                mag = s_mag[:, c:c + 1].to_broadcast([P, T])
                for k in range(2):
                    link(v.tensor_tensor_scan(tmp[:, 8 + k, :], mag, tmp[:, 2 * k, :], 0.0, ALU.mult, ALU.add))
                if c >= 2:
                    tile_used(ve, tile_at("ssm", c - 2))
                for k, (src, tab) in enumerate(((8, cc), (9, ss), (8, ss), (9, cc))):
                    link(TT(tmp[:, 10 + k, :], tmp[:, src, :], tab, ALU.mult))
                TT(ssm_s[:, 2 * (c % 2), :], tmp[:, 10, :], tmp[:, 11, :], ALU.subtract).then_inc(S("s_ready"), 1)
                STT(ssm_s[:, 2 * (c % 2) + 1, :], tmp[:, 12, :], -1.0, tmp[:, 13, :], ALU.mult, ALU.subtract)\
                    .then_inc(S("s_ready"), 1)
                if c % 4 == 0 and c:
                    skip(ve, c // 4 - 1)
            skip(ve, KS - 1)

            def glu(u, i):
                n = i * 4 + u
                b = block_at("glu", 3 * u, i, 12)
                block_here(ve, b)
                ve.wait_ge(S("glu_tanh"), n * 2 + 1)
                STT(tmp[:, 4 + u % 2, :], tmp[:, 2 * (u % 2), :], 1.0, bank(b), ALU.add, ALU.mult)\
                    .then_inc(S("glu_mul"), 1)
                ve.wait_ge(S("glu_mul"), n + 1)
                ve.wait_ge(S("glu_tanh"), n * 2 + 2)
                STT(pick(mg2, n), tmp[:, 2 * (u % 2) + 1, :], 1.0, tmp[:, 4 + u % 2, :], ALU.add, ALU.mult)\
                    .then_inc(S("glu_done"), 1)
            rounds(ve, KD, 4, glu)

            b = block_at("f", 0)
            block_here(ve, b)
            TS(fl[0], psum[0:HEADS, b.slot, :], V("fbias")[0:HEADS, :], None, ALU.add).then_inc(S("f_read"), 1)
            ve.wait_ge(S("f_read"), 1)
            STT(fl[2], fl[0], -1.0, fl[0], ALU.mult, ALU.max).then_inc(S("f_abs"), 1)
            ve.wait_ge(S("f_act"), 1)
            TS(fl[3], fl[1], 1.0, None, ALU.add).then_inc(S("f_one"), 1)
            ve.wait_ge(S("f_one"), 1)
            ve.wait_ge(S("f_act"), 2)
            log1p_exp(fl[2], fl[1], fl[3], fl[4], fl[5], fl[6])
            link(TS(fl[5], fl[0], 0.0, -1.0, ALU.min, ALU.mult))
            link(TT(fl[6], fl[6], fl[5], ALU.add))
            link(v.memset(fl[7], 1.0))
            v.tensor_tensor_scan(cumn, fl[7], fl[6], 0.0, ALU.mult, ALU.add).then_inc(S("cum_ready"), 1)

            link(TS(dcol[:, 0:1], V("qg"), HEAD_SCALE, None, ALU.mult))
            for n in range(2 * HEADS):
                dst = (qT if n < HEADS else kT)[:, n % HEADS, :]
                g = dcol[:, 0:1] if n < HEADS else V("kg")
                ve.wait_ge(S("hsd_done"), n + 1)
                link(v.reciprocal(tmp[:, 4 + n % 2, :], tmp[:, 2 + n % 2, :]))
                ve.wait_ge(S("hss_done"), n + 1)
                STT(dst, dst, g, tmp[:, 4 + n % 2, :], ALU.mult, ALU.mult).then_inc(S("qk_normed"), 1)

            for hd in range(HEADS):
                at = NB * (hd % 2)
                for qb in range(NB):
                    b = block_at("attn", 9 * hd + qb)
                    block_here(ve, b)
                    v.tensor_reduce(nmx[:, at + qb:at + qb + 1], bank(b, (qb + 1) * P), AX, ALU.max, negate=True)\
                        .then_inc(S("amax"), 1)
                for qb in range(NB):
                    ve.wait_ge(S("p_exp"), NB * hd + qb + 1)
                    link(v.reciprocal(rrs[:, at + qb:at + qb + 1], rs[:, at + qb:at + qb + 1]))
                    TS(probs[:, qb, 0:(qb + 1) * P], probs[:, qb, 0:(qb + 1) * P], rrs[:, at + qb:at + qb + 1], None,
                       ALU.mult).then_inc(S("p_ready"), 1)
                if hd:
                    block_here(ve, block_at("attn", 9 * (hd - 1) + 2 * NB))
                for kb in range(NB):
                    b = block_at("attn", 9 * hd + NB + kb)
                    block_here(ve, b)
                    v.tensor_copy(probsT[:, kb, kb * P:T], psum[:, b.slot, kb * P:T]).then_inc(S("pt_ready"), 1)

            def ga(u, i):
                n = i * 4 + u
                ve.wait_ge(S("ga_tanh"), n + 1)
                STT(tmp[:, 10 + u % 2, :], tmp[:, 8 + u % 2, :], 1.0, pick(y, n), ALU.add, ALU.mult)\
                    .then_inc(S("ga_mul"), 1)
                ve.wait_ge(S("ga_mul"), n + 1)
                STT(pick(mg2, n), pick(mg2, n), 0.5, tmp[:, 10 + u % 2, :], ALU.mult, ALU.add)\
                    .then_inc(S("merged2"), 1)
            ve.wait_ge(S("o_ready"), HEADS)
            rounds(ve, KD, 4, ga)
            rounds(ve, KD, 4, add_to_x("out2", "x_mixed2", lambda n: 0.5))
            ve.wait_ge(S("x_mixed2"), KD)
            norm(4, x, h2, T, V("ffng"), None)

            def top16(vals, idx, src, w):
                link(v.max(vals[:, 0:8], src))
                link(v.max_index(idx[:, 0:8], vals[:, 0:8], src))
                link(v.match_replace(scratch[:, 0:w], vals[:, 0:8], src, NEG))
                link(v.max(vals[:, 8:16], scratch[:, 0:w]))
                return v.max_index(idx[:, 8:16], vals[:, 8:16], scratch[:, 0:w])
            for n in range(16):
                ve.wait_ge(S("sc_ready"), n + 1)
                for tb in range(NB):
                    at = n * TOPK
                    last = top16(tops[:, tb, at:at + TOPK], topi[:, tb, at:at + TOPK].bitcast(U32),
                                 tmp[:, n % 4, tb * P:(tb + 1) * P], P)
                    if tb == NB - 1:
                        last.then_inc(S("topk_done"), 1)
                    else:
                        link(last)
            ve.wait_ge(S("topk_done"), 16)
            for tb in range(NB):
                link(v.tensor_copy(topf[:, tb, :], topi[:, tb, :].bitcast(U32)))
            for tb in range(NB):
                for hd in range(PH):
                    s0 = tops[:, tb, 2 * hd * TOPK:(2 * hd + 1) * TOPK]
                    s1 = tops[:, tb, (2 * hd + 1) * TOPK:(2 * hd + 2) * TOPK]
                    link(TT(t3(cand, TOPK), s0.unsqueeze(2).to_broadcast([P, TOPK, TOPK]),
                            s1.unsqueeze(1).to_broadcast([P, TOPK, TOPK]), ALU.add))
                    link(top16(best[:, hd * TOPK:(hd + 1) * TOPK], posn[:, hd * TOPK:(hd + 1) * TOPK].bitcast(U32),
                               cand, TOPK * TOPK))
                b3 = t3(best, TOPK)
                TT(t3(fa, TOPK), b3, b3[:, :, 0:1].to_broadcast([P, PH, TOPK]), ALU.subtract)\
                    .then_inc(S("best_ready"), 1)
                link(TS(posa.bitcast(U32), posn.bitcast(U32), 4, None, ALU.logical_shift_right))
                link(TS(posb.bitcast(U32), posn.bitcast(U32), TOPK - 1, None, ALU.bitwise_and))
                ve.wait_ge(S("best_exp"), tb + 1)
                link(v.tensor_reduce(gsum, t3(bexp, TOPK), AX, ALU.add))
                link(v.reciprocal(grec, gsum))
                link(TT(t3(picks[:, tb, 2 * P:3 * P], TOPK), t3(bexp, TOPK),
                        grec.unsqueeze(2).to_broadcast([P, PH, TOPK]), ALU.mult))
                for half, pos in enumerate((posa, posb)):
                    link(v.tensor_copy(fb, pos.bitcast(U32)))
                    e4 = eq.rearrange("p (k c) -> p k c", c=TOPK)
                    link(TT(e4, iota[:, 0:TOPK].unsqueeze(1).to_broadcast([P, P, TOPK]),
                            fb.unsqueeze(2).to_broadcast([P, P, TOPK]), ALU.is_equal))
                    key = topf[:, tb, :].rearrange("p (h two c) -> p h two c", two=2, c=TOPK)[:, :, half, :]
                    link(TT(prod.rearrange("p (h k c) -> p h k c", h=PH, c=TOPK),
                            eq.rearrange("p (h k c) -> p h k c", h=PH, c=TOPK),
                            key.unsqueeze(2).to_broadcast([P, PH, TOPK, TOPK]), ALU.mult))
                    link(v.tensor_reduce(picks[:, tb, half * P:(half + 1) * P],
                                         prod.rearrange("p (k c) -> p k c", c=TOPK), AX, ALU.add))
                ve.sem_inc(S("picks_ready"), 1)

            def spread(u, i):
                n = i * 4 + u
                if isinstance(i, int) and n < 2:
                    pass
                else:
                    ve.wait_ge(S("pe_done"), block_at("gate", u, i, 4).of(DONE, 2) if not isinstance(i, int)
                               else DONE[BLOCK0["gate"] + n - 2])
                for k in range(4):
                    t = n * 4 + k
                    TS(hot_a[:, u % 2, k * P:(k + 1) * P], iota[:, :], col(picksT[:, 0, :], t),
                       col(picksT[:, 2, :], t), ALU.is_equal, ALU.mult)
                    last = TS(hot_b[:, u % 2, k * P:(k + 1) * P], iota[:, :], col(picksT[:, 1, :], t), None,
                              ALU.is_equal)
                last.then_inc(S("hot_ready"), 1)
            ve.wait_ge(S("picksT_ready"), NB)
            rounds(ve, T // 4, 4, spread)

            def group(i):
                ve.wait_ge(S("gates_back"), i * 16 + 16)
                wait(ve, S("eo_done"), i * KD)
                for k in range(JG):
                    ve.wait_ge(S("ea_ready"), i * JG + (k + 1))
                    TT(ew[:, k, :], tmp[:, k % 4, :], gbuf[:, k, :], ALU.mult).then_inc(S("ew_ready"), 1)
                for dc in range(KD):
                    ve.wait_ge(S("eo_done"), i * KD + (dc + 1))
                    wait(ve, S("eo_read"), i * KD)
                    TT(x[:, dc, :], x[:, dc, :], psum[:, 4 + dc % 4, :], ALU.add).then_inc(S("eo_read"), 1)
            group(0)
            with ve.Fori(1, PK // JG) as i:
                group(i)

        @block.gpsimd
        def _(gp):
            g = nc.gpsimd
            g.memset(ones[:, :], 1.0).then_inc(S("consts_ready"), 1)
            g.iota(iota[:, :], [[1, P]], base=0, channel_multiplier=0, allow_small_or_imprecise_dtypes=True)\
                .then_inc(S("consts_ready"), 1)
            g.memset(ident[:, :], 0.0).then_inc(S("consts_ready"), 1)
            gp.wait_ge(S("consts_ready"), 3)
            g.affine_select(out=ident[:, :], in_=ident[:, :], compare_op=ALU.not_equal, fill=1.0, base=0,
                            pattern=[[-1, P]], channel_multiplier=1).then_inc(S("consts_ready"), 1)
            gp.wait_ge(S("lru_done"), 2 * NR)
            g.memset(maskt, 0.0).then_inc(S("mask_zero"), 1)
            g.memset(sel, 0.0).then_inc(S("mask_zero"), 1)
            gp.wait_ge(S("mask_zero"), 2)
            g.affine_select(out=maskt, in_=maskt, compare_op=ALU.is_ge, fill=NEG, base=0, pattern=[[-1, P]],
                            channel_multiplier=1).then_inc(S("mask_ready"), 1)
            g.affine_select(out=sel, in_=sel, compare_op=ALU.not_equal, fill=1.0, base=0,
                            pattern=[[-1, HEADS], [0, P]], channel_multiplier=1).then_inc(S("mask_ready"), 1)


HEAD_SCALE = float(P) ** -0.5


def _two_pi_parts():
    out, rest = [], TWO_PI
    for bits in (9, 11):
        scale = 2.0 ** (bits - math.ceil(math.log2(rest)))
        out.append(math.floor(rest * scale) / scale)
        rest -= out[-1]
    return out + [float(np.float32(rest))]


TWO_PI_PARTS = _two_pi_parts()


def _tiles(w):
    k, n = w.shape
    return w.reshape(k // P, P, n // P, P).transpose(2, 1, 0, 3).reshape(n // P, P, k)


def _wide_tiles(w):
    return w.reshape(4, 2, P, 2, 512).transpose(3, 0, 2, 1, 4).reshape(8, P, 1024)


def _cols(v):
    return v.reshape(-1, P).T


def kernel(**inputs):
    from concourse import bacc
    from concourse.bass_utils import run_bass_kernel_spmd

    a = {k: np.asarray(v) for k, v in inputs.items()}
    arrays = {}

    def put(name, v):
        arrays[name] = np.ascontiguousarray(v)

    xT = a["x"][0].T.reshape(KD, P, T).transpose(1, 0, 2)
    cT = a["ctx"][0].T.reshape(KD, P, TC).transpose(1, 0, 2)
    put("xT", xT)
    put("xc", np.concatenate([xT, cT], axis=2))
    wm, w_in = a["w_mod"][0], a["w_in"][0]
    put("w_moda", _tiles(wm[:, :2048]))
    put("w_modb", _tiles(wm[:, 2048:]))
    offs = np.cumsum([0, W_R, W_R, W_G, W_G, D, D])
    rx, rg, uu, vv, gr, gg = (w_in[:, lo:hi] for lo, hi in zip(offs[:-1], offs[1:]))
    put("w_rx", _tiles(rx))
    put("w_rg", _tiles(rg))
    put("w_u", _tiles(uu))
    put("w_v", _wide_tiles(vv))
    put("w_gr", _tiles(gr))
    put("w_gg", _tiles(gg))
    wa, wx = a["lru_wa"][0], a["lru_wx"][0]
    both = np.stack([wa, wx], axis=0).reshape(2, 2, 5, 2, P, 2, P)
    put("w_gates", both.transpose(1, 2, 5, 4, 0, 3, 6).reshape(2 * NR, P, 4 * P))
    put("w_sT", a["w_s"][0].transpose(2, 0, 1).reshape(P, HG * P))
    put("bsrow", np.broadcast_to(a["b_s"][0].T[None], (P, HG, P)))
    put("w_pr", _tiles(a["w_pr"][0]))
    put("w_pg", _tiles(a["w_pg"][0]))
    put("w_out", _tiles(a["w_out"][0]))
    up = a["w_up"][0]
    put("w_up", np.stack([_tiles(up[:, :D_FF]), _tiles(up[:, D_FF:])], axis=1).reshape(2 * NF, P, D))
    put("w_down", _tiles(a["w_down"][0]).reshape(KD, P, 2, SLOT).transpose(0, 2, 1, 3).reshape(2 * KD, P, SLOT))
    w2 = a["w_in_2"][0]
    o = np.cumsum([0, SSM, D, D, D, HEADS, D, D])
    wu, wq, wk, wv, wf, wgs, wga = (w2[:, lo:hi] for lo, hi in zip(o[:-1], o[1:]))
    put("w_u2", _tiles(wu))
    put("w_q", _tiles(wq))
    put("w_k", _tiles(wk))
    put("w_v2", _wide_tiles(wv))
    put("w_f", wf.reshape(KD, P, HEADS).transpose(1, 0, 2).reshape(P, KD * HEADS))
    put("w_ga", _tiles(wga))
    glu = a["ssm_w_glu_2"][0]
    vg = np.concatenate([_tiles(glu[:, :D]), _tiles(glu[:, D:])], axis=2)
    put("w_glu", np.stack([vg, _tiles(wgs)], axis=1).reshape(2 * KD, P, D))
    put("w_out2", _tiles(a["w_out_2"][0]))
    put("w_query", _tiles(a["peer_w_query_2"][0]))
    sk = a["peer_sub_keys_2"][0].reshape(16, PK, P)
    put("w_keys", sk.transpose(2, 0, 1).reshape(P, 2, 8 * P).transpose(1, 0, 2))
    ssm = np.zeros((NS, P, 4, P), np.float32)
    for k, name in enumerate(("ssm_b_re_2", "ssm_b_im_2", "ssm_c_re_2", "ssm_c_im_2")):
        w = a[name][0] if k < 2 else a[name][0].transpose(0, 2, 1)
        for g in range(32):
            c, r = g // 2, g % 2
            f0 = 32 * (c % 4) + 16 * r
            ssm[c, 64 * r:64 * r + 64, k, f0:f0 + 16] = w[g]
    put("w_ssm", ssm.reshape(NS, P, 4 * P))
    put("u_tab", a["peer_u_2"][0].reshape(PK, PK, KD, P).transpose(1, 3, 2, 0).reshape(PK, P, D))
    put("v_tab", a["peer_v_2"][0].reshape(PK, PK // JG, JG, D).transpose(1, 0, 2, 3))

    v = {"c2": np.stack([a["c"][0].reshape(KD, P), a["c_ctx"].reshape(KD, P)], axis=1).reshape(16, P).T,
         "bmod": _cols(a["b_mod"][0]), "g1": _cols(a["g_norm1"][0]),
         "convw": a["conv_w"][0].reshape(KR, NR, P).transpose(2, 1, 0).reshape(P, NR * KR),
         "convb": _cols(a["conv_b"][0]), "lam": _cols(a["lru_lam"][0].reshape(-1)),
         "ba": _cols(a["lru_ba"][0].reshape(-1)), "bx": _cols(a["lru_bx"][0].reshape(-1)),
         "gv": _cols(a["g_v"][0]), "g2": _cols(a["g_norm2"][0]),
         "fcw": a["ffn_conv_w"][0].reshape(9, NF, P).transpose(2, 1, 0).reshape(P, NF * 9),
         "fcb": _cols(a["ffn_conv_b"][0]), "gfin": _cols(a["g_final"]), "mixg": _cols(a["mix_norm_g_2"][0]),
         "are": _cols(a["ssm_a_re_2"][0].reshape(-1)), "aim": _cols(a["ssm_a_im_2"][0].reshape(-1)),
         "lstep": _cols(np.repeat(a["ssm_log_step_2"][0], 64)), "dskip": _cols(a["ssm_d_2"][0]),
         "fbias": np.concatenate([a["fox_forget_bias_2"][0], np.zeros(P - HEADS, np.float32)])[:, None],
         "qg": a["q_norm_g_2"][0][:, None], "kg": a["k_norm_g_2"][0][:, None], "ffng": _cols(a["ffn_norm_g_2"][0]),
         "eps": np.full((P, 1), EPS, np.float32)}
    put("vecs", np.concatenate([v[n] for n, _ in VECS], axis=1))

    nc = bacc.Bacc("TRN2", target_bir_lowering=False, num_devices=1)
    io = {k: nc.dram_tensor(k, w.shape, F32, kind="ExternalInput").ap() for k, w in arrays.items()}
    io["out"] = nc.dram_tensor("out", (D, T), F32, kind="ExternalOutput").ap()
    build(nc, io)
    r = run_bass_kernel_spmd(nc, [arrays], core_ids=[0])
    return r.results[0]["out"].T.reshape(1, T, D)
```

```python
import math
from contextlib import ExitStack

import numpy as np

import concourse.bass as bass
from concourse import mybir

F32 = mybir.dt.float32
F32R = mybir.dt.float32r
U32 = mybir.dt.uint32
ACT = mybir.ActivationFunctionType
ALU = mybir.AluOpType
AX = mybir.AxisListType.X

P = 128
T, TC = 512, 256
TX = T + TC
D = 1024
KD = D // P
W_R = 1280
NR = W_R // P
KR = 4
W_G = 1024
HG = 8
D_FF = 2816
NF = D_FF // P
NFH = NF // 2
GW = 64
GH = T // GW
EPS = 1e-6
SSM = 512
KS = SSM // P
NS = 16
HEADS = 8
PH, PK, TOPK = 8, 128, 16
R = 4
SLOT = 11 * P
NB = T // P
JG = 8
TG = 64
TWO_PI = 2.0 * math.pi
ROUND = 1.5 * 2.0 ** 23
PI_LESS = 3.1415925
NEG = -1e30

VECS = [("c2", 2 * KD), ("bmod", 48), ("g1", KD), ("convw", NR * KR), ("convb", NR), ("lam", 2 * NR),
        ("ba", 2 * NR), ("bx", 2 * NR), ("gv", HG), ("g2", KD), ("fcw", NF * 9), ("fcb", NF), ("gfin", KD),
        ("mixg", KD), ("are", NS), ("aim", NS), ("lstep", NS), ("dskip", KS), ("fbias", 1), ("qg", 1),
        ("kg", 1), ("ffng", KD), ("eps", 1)]
VCOL, _at = {}, 0
for _n, _w in VECS:
    VCOL[_n] = _at
    _at += _w
NVEC = _at

MODB = [32 * n // (2 * NR) for n in range(2 * NR + 1)]
LRU_STAGES = []
for _n in range(2 * NR):
    LRU_STAGES += [(f"gates{_n}", 1, ["B", "B", "B", "BT"], lambda j, n=_n: ("gate_tanh", 4 * n + j + 1)),
                   (f"modb{_n}", MODB[_n + 1] - MODB[_n], ["T"], None)]
STAGES = [
    ("moda", 16, ["T"], None),
    ("rx", NR, ["B", "BT"], lambda j: ("pad_ready", j + 1)),
    *LRU_STAGES,
    ("rg", NR, ["BT"], lambda j: ("rg_gelu", j + 1)),
    ("v", 8, ["T"], None),
    ("mix", 1, ["B"] * (HG - 1) + ["BT"], lambda j: ("yg_mixed", j + 1)),
    ("u", HG, ["BT"], lambda j: ("u_gelu", j + 1)),
    ("merge", KD, ["BT"] * 4, lambda j: (("merge_tanh", "merge_mul")[j % 2], 2 * (j // 4) + 1 + j % 4 // 2)),
    ("out", KD, ["BT"], lambda j: ("x_mixed", j + 1)),
    ("up0", NFH, ["BT", "BT"], lambda j: (("ffpad_ready", "ff_used")[j % 2], j // 2 + 1)),
    ("down0", KD, ["BT"], lambda j: ("x_ffn", j + 1)),
    ("up1", NFH, ["BT", "BT"], lambda j: (("ffpad_ready", "ff_used")[j % 2], NFH + j // 2 + 1)),
    ("down1", KD, ["BT"], lambda j: ("x_ffn", KD + j + 1)),
    ("u2", KS, ["BT"], lambda j: ("u2_ready", j + 1)),
    ("ssm", NS, ["T"], None),
    ("glu", KD, ["B", "BT", "BT"],
     lambda j: ("glu_mul", j // 3 + 1) if j % 3 == 0 else ("glu_tanh", 2 * (j // 3) + j % 3)),
    ("q", KD, ["BT"], lambda j: ("q_ready", j + 1)),
    ("k", KD, ["BT"], lambda j: ("k_ready", j + 1)),
    ("v2", 8, ["T"], None),
    ("f", 1, ["BT"], lambda j: ("f_read", 1)),
    ("attn", HEADS, ["B"] * (2 * NB + 1),
     lambda j: [("p_exp", NB * (j // 9) + j % 9 + 1), ("pt_ready", NB * (j // 9) + j % 9 - NB + 1),
                ("o_ready", j // 9 + 1)][j % 9 // NB]),
    ("ga", KD, ["BT"], lambda j: ("ga_tanh", j + 1)),
    ("out2", KD, ["BT"], lambda j: ("x_mixed2", j + 1)),
    ("query", 16, ["BT"], lambda j: ("pq_ready", j + 1)),
    ("keys", 2, ["B"] * 7 + ["BT"], lambda j: ("sc_ready", j + 1)),
    ("gate", T // 4, ["B"], lambda j: ("gates_staged", j + 1)),
    ("experts", 2 * PK, ["T"], None),
]
WHOLE = {"moda", "mix", "ssm", "f", "keys"} | {stage[0] for stage in LRU_STAGES}
TILE0, BLOCK0, USED, DONE, READ = {}, {}, [], [], []
SPLIT0, SPLIT_USED, FREED = {}, [], []
_count = 0
for _name, _units, _signals, _reader in STAGES:
    TILE0[_name], BLOCK0[_name], SPLIT0[_name] = len(USED), len(DONE), len(SPLIT_USED)
    for _k in range(_units * len(_signals)):
        _count += 1
        if "T" in _signals[_k % len(_signals)]:
            USED.append(_count)
            if _name in WHOLE:
                FREED.append(("pe_done", _count))
            else:
                SPLIT_USED.append(_count)
                FREED.append(("split_ready", len(SPLIT_USED)))
        if "B" in _signals[_k % len(_signals)]:
            READ.append(_reader(len(DONE) - BLOCK0[_name]))
            DONE.append(_count)


class At:

    def __init__(self, first, i=0, step=0):
        assert step % R == 0
        self.first, self.i, self.step = first, i, step
        self.slot = first % R
        self.turn = i * (step // R) + first // R
        self.count = i * step + first
        self.fresh = isinstance(i, int) and first + i * step < R

    def of(self, table, back=0):
        first = self.first - back
        if isinstance(self.i, int):
            return table[first + self.i * self.step]
        one, two = table[first + self.step], table[first + 2 * self.step]
        return self.i * (two - one) + (2 * one - two)


def rounds(eng, n, per, body):
    whole = n // per
    if whole >= 3:
        for u in range(per):
            body(u, 0)
        with eng.Fori(1, whole) as i:
            for u in range(per):
                body(u, i)
    else:
        for i in range(whole):
            for u in range(per):
                body(u, i)
    for u in range(n % per):
        body(u, whole)


def grouped(eng, n, per, body):
    rounds(eng, n - n % per, per, lambda u, i: body(range(per), i) if u == 0 else None)
    if n % per:
        body(range(n % per), n // per)


def wait(eng, sem, value):
    if not isinstance(value, int) or value > 0:
        eng.wait_ge(sem, value)


def chain(eng, sem, base=0):
    done = [0]

    def link(ins):
        done[0] += 1
        ins.then_inc(sem, 1)
        eng.wait_ge(sem, base + done[0])
        return ins
    return link


def lanes(eng, sem, count, base=0):
    done = [0]

    def link(ins):
        done[0] += 1
        ins.then_inc(sem, 1)
        wait(eng, sem, base + done[0] - count + 1)
        return ins
    return link


def build(nc, io):
    with ExitStack() as ctx:
        sems = {}

        def S(name):
            if name not in sems:
                sems[name] = ctx.enter_context(nc.semaphore(name))
            return sems[name]

        def sb(name, cols, dt=F32):
            return ctx.enter_context(nc.sbuf_tensor(name, [P, cols], dt))

        ring_t = sb("ring", R * SLOT)
        wh_t, wl_t = sb("wh", 2 * SLOT, F32R), sb("wl", 2 * SLOT, F32R)
        vec, mod_t, small = sb("vec", NVEC), sb("mod", 96), sb("small", 1024)
        ones, ident, iota, maskt = sb("ones", P), sb("ident", P), sb("iota", P), sb("mask", P)
        ARENA = 39400
        base = 4 * (-(-nc.sbuf_base // 32) * 8)
        sb("arena", ARENA)
        B = 12288

        def ar(name, at, chunks, w=T, dt=F32):
            assert at + chunks * w <= ARENA
            t = nc.alloc_sbuf_tensor_at(name, [P, chunks * w], dt, offset=base + 4 * at)
            return t[:, :].rearrange("p (c w) -> p c w", w=w)

        psum = ctx.enter_context(nc.psum_tensor("psum", [P, 8, T], F32))
        gates_d = nc.dram_tensor("gates_scratch", (P, PK, T), F32, kind="Internal").ap()

        def view(t, at, c, w):
            return t[:, at:at + c * w].rearrange("p (c w) -> p c w", w=w)

        def pick(t, n):
            if isinstance(n, int):
                return t[:, n, :]
            return t[:, bass.ds(n, 1), :].rearrange("p o w -> p (o w)")

        def dram(name, n):
            if isinstance(n, int):
                return io[name][n]
            return io[name][bass.ds(n, 1)].rearrange("o p w -> p (o w)")

        def col(t, n):
            return t[:, n:n + 1] if isinstance(n, int) else t[:, bass.ds(n, 1)]

        def V(name):
            return vec[:, VCOL[name]:VCOL[name] + dict(VECS)[name]]

        taken = [0]

        def sm(w, dt=F32):
            a = small[:, taken[0]:taken[0] + w]
            taken[0] += w
            assert taken[0] <= 1024
            return a

        def t3(a, w):
            return a.rearrange("p (c w) -> p c w", w=w)

        def both(name, at, chunks, w=T):
            return ar(name + "_hi", at, chunks, w, F32R), ar(name + "_lo", at + chunks * w, chunks, w, F32R)

        mod = mod_t[:, :].rearrange("p (n k) -> p n k", k=2)
        x = ar("x", 0, KD)
        h = both("h", 4096, KD)
        xc, hc = ar("xc", B, KD, TX), both("hc", B + 6144, KD, TC)
        nrm = [[ar(f"n{j}_{k}", at + k * w, 1, w)[:, 0, :] for k in range(6)]
               for j, (at, w) in enumerate(((B + 10240, TX), (B + 23552, T), (B + 23552, T), (B + 23552, T),
                                            (B + 18432, T)))]
        pads = [ar(f"pad{k}", B + 14848 + k * 784, 1, 774)[:, 0, :] for k in range(2)]
        xr = ar("xr", B + 17000, NR, TX)
        lw, la, lb = (ar(name, B + 5120 + k * 5 * TX, 5, TX) for k, name in enumerate(("lw", "la", "lb")))
        y = ar("y", B, NR)
        rr, ri, lq = ar("rr", 0, 2, TX), ar("ri", 2 * TX, 2, TX), ar("lq", B + 24680, 1, TX)[:, 0, :]
        cs, yb = ar("cs", 4 * TX, 1, TC)[:, 0, :], ar("yb", 4 * TX + TC, 1)[:, 0, :]
        yr = both("yr", B + 5120, NR)
        gt = ar("gt", B + 24680, 4)
        vtok, yg, bsrow = ar("vtok", B + 15360, NB, W_G), ar("yg", B, HG), ar("bsrow", B + 4096, HG, P)
        vjunk = ar("vjunk", B + 19456, 1, W_G)[:, 0, :]
        ygs = both("ygs", B + 15360, HG)
        mg, mt, mgs = ar("mg", B, KD), ar("mt", B + 23552, 4), both("mgs", B + 5120, KD)
        ffs = both("ffs", B, NFH)
        ffp = [ar(f"ffpad{k}", B + 11264 + 672 * k, GH + 2, GW + 2) for k in range(2)]
        fcv, fge, fra = (ar(n, B + 17104 + k * 1024, 2) for k, n in enumerate(("fcv", "fge", "fra")))
        tables = [(ar(f"cos{k}", at, n), ar(f"sin{k}", at + n * T, n), ar(f"trigw{k}", work, n // 2), first, n)
                  for k, (at, work, first, n) in enumerate(((B + 11264, 4096, 0, 12), (B, B + 6656, 12, 4)))]
        ysh, ysl = ar("ys_hi", B + 11264, KS, T, F32R), ar("ys_lo", B + 17408, KS, T, F32R)
        u2, st, ssm_s = ar("u2", B + 8192, KS), ar("st", B + 23552, 6), ar("ss", B + 4096, 4)
        ysk, back = ar("ysk", B + 6144, 1)[:, 0, :], ar("back", B + 6656, 2)
        bw, bt = ar("bw", B + 10240, 2, 2 * P), ar("bt", B + 10752, 2, 2 * P)
        bt1, bt2 = (ar(f"bt{k}", B + 7680 + P * k, 1, P)[:, 0, :] for k in range(2))
        mg2, mg2s = ar("mg2", B + 2048, KD), both("mg2s", B + 10240, KD)
        gl = ar("gl", B + 21504, 6)
        qT, kT, vt2 = ar("qT", B + 6144, HEADS), ar("kT", B + 10240, HEADS), ar("vt2", B + 14336, NB, D)
        ht = ar("ht", B + 18432, 6)
        fl = [ar(f"fl{k}", B + (k * T if k < 4 else 21504 + (k - 4) * T), 1)[0:HEADS, 0, :] for k in range(8)]
        sel, cumn = ar("sel", B + 25344, HEADS, P), ar("cumn", B + 26368, 1)[0:HEADS, 0, :]
        probs, probsT = ar("probs", B + 18432, NB), ar("probsT", B + 20480, NB)
        gat = ar("gat", B + 22528, 4)
        pq, scb = ar("pq", B, 16), ar("scb", B + 8192, 4)
        tops, topi, topf = (ar(n, B + 10240 + k * 1024, NB, 16 * TOPK) for k, n in
                            enumerate(("tops", "topi", "topf")))
        picks = ar("picks", B + 13312, NB, 3 * P)
        spare, cand = ar("spare", B + 22032, 4, 256), ar("cand", B + 23056, 4, 256)
        best, posn, posa, posb, bexp, fa, fb = (
            ar(n, B + 15360 + k * P, 1, P)[:, 0, :] for k, n in
            enumerate(("best", "posn", "posa", "posb", "bexp", "fa", "fb")))
        eq, prod = (ar(n, B + 16400 + k * 2048, 1, 2048)[:, 0, :] for k, n in enumerate(("eq", "prod")))
        picksT = ar("picksT", B + 20496, 3)
        hot_a, hot_b = ar("hot_a", B + 22032, 4), ar("hot_b", B + 24080, 4)
        stage = [ar(f"stage{k}", B + k * PK * TG, PK, TG) for k in range(2)]
        gbuf, ews = ar("gbuf", B, JG), both("ews", B + 4096, JG)
        ga4, er = ar("ga4", B + 22032, 4), ar("er", B + 24080, 2)
        silu = t3(sm(2 * KD), 2)
        a1, a2 = t3(sm(2 * KD), 2), sm(KD)
        hm2 = sm(KD)
        sp = [sm(2 * NR) for _ in range(6)]
        sp2, sp4n, hba, hbx = (sm(2 * NR) for _ in range(4))
        vss, vsd, vrs = sm(NB), sm(NB), sm(NB)
        sc = [sm(NS) for _ in range(12)]
        s_step, s_mag, s_cos, s_sin = (sm(NS) for _ in range(4))
        cr, ci = sm(NS), sm(NS)
        pw = sm(10 * 2 * NS).rearrange("p (l k s) -> p l k s", k=2, s=NS)
        nmx, rs, rrs = sm(2 * NB), sm(2 * NB), sm(2 * NB)
        dcol, gsum, grec = sm(KS), sm(PH), sm(PH)
        share4 = t3(sm(16), 4)

        def slot(at, lo, n):
            return ring_t[:, at.slot * SLOT + lo:at.slot * SLOT + lo + n]

        def wchunk(at, k, w=P):
            return slot(at, k * w, w)

        def whl(s, k, w=P):
            at = (s.first % 2) * SLOT + k * w
            return wh_t[:, at:at + w], wl_t[:, at:at + w]

        def bank(at, n=T):
            return psum[:, at.slot, 0:n]

        def tile_at(stage, k, i=0, step=0):
            return At(TILE0[stage] + k, i, step)

        def split_at(stage, k, i=0, step=0):
            return At(SPLIT0[stage] + k, i, step)

        def block_at(stage, k, i=0, step=0):
            return At(BLOCK0[stage] + k, i, step)

        def tile_here(eng, at):
            eng.wait_ge(S(f"tile_loaded{at.slot}"), at.turn * 16 + 16)

        def freed(eng, at, table):
            if not at.fresh:
                name = table[at.first - R + (at.step if not isinstance(at.i, int) else at.i * at.step)][0]
                eng.wait_ge(S(name), at.of([r[1] for r in table], R))

        def block_free(eng, at):
            freed(eng, at, READ)

        def split_here(eng, s):
            eng.wait_ge(S("split_ready"), s.count + 1)

        def block_here(eng, at):
            eng.wait_ge(S("pe_done"), at.of(DONE))

        def tile_used(eng, at):
            eng.wait_ge(S("pe_done"), at.of(USED))

        def skip(ve, oc):
            tile_used(ve, tile_at("ssm", 4 * oc + 3))
            nc.vector.scalar_tensor_tensor(ysk, u2[:, oc, :], V("dskip")[:, oc:oc + 1],
                                           psum[:, 7, :], ALU.mult, ALU.add).then_inc(S("ys_read"), 1)

        block = ctx.enter_context(nc.Block())

        @block.sync
        def _(sp):
            def fetch(at, src, n):
                freed(sp, at, FREED)
                sp.dma_start(slot(at, 0, n), src).then_inc(S(f"tile_loaded{at.slot}"), 16)

            def stream(stage, name, n, size, per=4, first=0):
                def body(u, i):
                    fetch(tile_at(stage, u, i, per), dram(name, i * per + (u + first)), size)
                rounds(sp, n, per, body)

            sp.dma_start(vec[:, :], io["vecs"]).then_inc(S("vecs_loaded"), 16)
            sp.dma_start(xc, io["xc"]).then_inc(S("x_loaded"), 16)
            stream("moda", "w_moda", 16, KD * P)
            stream("rx", "w_rx", NR, KD * P)
            for n in range(2 * NR):
                fetch(tile_at(f"gates{n}", 0), dram("w_gates", n), 4 * P)
                for k in range(MODB[n], MODB[n + 1]):
                    fetch(tile_at(f"modb{n}", k - MODB[n]), dram("w_modb", k), KD * P)
            stream("rg", "w_rg", NR, KD * P)
            stream("v", "w_v", 8, 2 * 512)
            fetch(tile_at("mix", 0), io["w_sT"], HG * P)
            sp.wait_ge(S("lru_done"), 2 * NR)
            sp.dma_start(x, io["xT"]).then_inc(S("xres_loaded"), 16)
            sp.wait_ge(S("yr_ready"), NR)
            sp.dma_start(bsrow, io["bsrow"]).then_inc(S("bsrow_loaded"), 16)
            stream("u", "w_u", HG, KD * P)

            def merge(u, i):
                for k, (name, c) in enumerate((("w_gr", KD), ("w_pr", NR), ("w_gg", KD), ("w_pg", KD))):
                    fetch(tile_at("merge", k, i, 4), dram(name, i), c * P)
            rounds(sp, KD, 1, merge)
            stream("out", "w_out", KD, KD * P)
            for k in range(2):
                stream(f"up{k}", "w_up", 2 * NFH, KD * P, first=k * 2 * NFH)
                stream(f"down{k}", "w_down", KD, SLOT, first=k * KD)
            stream("u2", "w_u2", KS, KD * P)
            stream("ssm", "w_ssm", NS, 4 * P)
            stream("glu", "w_glu", 2 * KD, KD * P)
            stream("q", "w_q", KD, KD * P)
            stream("k", "w_k", KD, KD * P)
            stream("v2", "w_v2", 8, 2 * 512)
            fetch(tile_at("f", 0), io["w_f"], KD * HEADS)
            stream("ga", "w_ga", KD, KD * P)
            stream("out2", "w_out2", KD, KD * P)
            stream("query", "w_query", 16, KD * P)
            stream("keys", "w_keys", 2, 8 * P)

            for k in range(R):
                fetch(tile_at("experts", k), dram("tables", k), D)
            for g in range(T // TG):
                sp.wait_ge(S("gates_staged"), (g + 1) * (TG // 4))
                sp.dma_start(gates_d[:, :, g * TG:(g + 1) * TG], stage[g % 2])\
                    .then_inc(S(f"gates_parked{g % 2}"), 16)
            for k in range(2):
                sp.wait_ge(S(f"gates_parked{k}"), 16 * (T // TG // 2))
            gd = gates_d.rearrange("p (g a) t -> g p a t", a=JG)

            def experts(i, first):
                wait(sp, S("ew_raw"), i * JG)
                sp.dma_start(gbuf, gd[i] if isinstance(i, int) else
                             gd[bass.ds(i, 1)].rearrange("o p a t -> p (o a) t")).then_inc(S("gates_back"), 16)
                for k in range(first, 2 * JG):
                    fetch(tile_at("experts", k, i, 2 * JG), dram("tables", i * 2 * JG + k), D)
            experts(0, R)
            with sp.Fori(1, PK // JG) as i:
                experts(i, 0)
            for n in range(KD):
                sp.wait_ge(S("eo_read"), (PK // JG - 1) * KD + n + 1)
                sp.dma_start(io["out"][n * P:(n + 1) * P, :], x[:, n, :]).then_inc(S("stored"), 16)
            sp.wait_ge(S("stored"), 16 * KD)

        @block.tensor
        def _(pe):
            PE = S("pe_done")

            def mm(out, lhsT, rhs, first, last, **kw):
                return nc.tensor.matmul(out, lhsT, rhs, start=first, stop=last, **kw)

            def passes(out, s, k, act, c, first, last, w=P):
                (wh, wl), (xh, xl) = whl(s, k, w), act
                mm(out, wh, xh[:, c, :], first, False)
                mm(out, wh, xl[:, c, :], False, False)
                return mm(out, wl, xh[:, c, :], False, last)

            def project(stage, n, per, act, kc=KD, ready=None, base=0):
                def body(u, i):
                    b, s = block_at(stage, u, i, per), split_at(stage, u, i, per)
                    block_free(pe, b)
                    split_here(pe, s)
                    for k in range(kc):
                        if ready and isinstance(i, int) and i == 0 and u == 0:
                            pe.wait_ge(S(ready), base + k + 1)
                        last = passes(bank(b), s, k, act, k, k == 0, k == kc - 1)
                    last.then_inc(PE, 1)
                rounds(pe, n, per, body)

            def norm(k, cols):
                wait(pe, S("sd_done"), k)
                for c in range(KD):
                    pe.wait_ge(S("sq_ready"), k * KD + c + 1)
                    sq = nrm[k][c % 2]
                    if cols > T:
                        mm(psum[:, 6, 0:cols - T], ones[:, :], sq[:, T:cols], c == 0, c == KD - 1)
                    mm(psum[:, 5, :], ones[:, :], sq[:, 0:T], c == 0, c == KD - 1).then_inc(S("sq_used"), 1)

            def modulation(stage, first, n):
                for u in range(n):
                    a = tile_at(stage, u)
                    tile_here(pe, a)
                    for k in range(KD):
                        last = mm(psum[:, 4, 2 * (first + u):2 * (first + u) + 2], wchunk(a, k),
                                  silu[:, k, :], k == 0, k == KD - 1)
                    last.then_inc(PE, 1)

            pe.wait_ge(S("consts_ready"), 4)
            norm(0, TX)
            pe.wait_ge(S("silu_ready"), 1)
            modulation("moda", 0, 16)

            def rx(u, i):
                s = split_at("rx", u, i, 4)
                b0, b1 = block_at("rx", 2 * u, i, 8), block_at("rx", 2 * u + 1, i, 8)
                split_here(pe, s)
                block_free(pe, b0)
                block_free(pe, b1)
                for k in range(KD):
                    last0 = passes(bank(b0), s, k, h, k, k == 0, k == KD - 1)
                    last1 = passes(bank(b1, TC), s, k, hc, k, k == 0, k == KD - 1)
                last0.then_inc(PE, 1)
                last1.then_inc(PE, 1)
            pe.wait_ge(S("norm_done"), KD)
            rounds(pe, NR, 4, rx)

            pe.wait_ge(S("xr_ready"), NR)
            pe.wait_ge(S("mod_read"), 1)
            for n in range(2 * NR):
                a = tile_at(f"gates{n}", 0)
                tile_here(pe, a)
                src = 2 * ((n % NR) // 2)
                for g in range(2):
                    for part, (lo, hi) in enumerate(((0, T), (T, TX))):
                        b = block_at(f"gates{n}", 2 * g + part)
                        block_free(pe, b)
                        for k in range(2):
                            last = mm(bank(b, hi - lo), wchunk(a, 2 * g + k), xr[:, src + k, lo:hi], k == 0, k == 1)
                        last.then_inc(PE, 1)

                modulation(f"modb{n}", 16 + MODB[n], MODB[n + 1] - MODB[n])

            project("rg", NR, 4, h)
            pe.wait_ge(S("mod_read"), 2)

            def token_major(stage, read):
                for half in range(2):
                    if half:
                        pe.wait_ge(S(read), NB)
                    for kg in range(4):
                        s = split_at(stage, 4 * half + kg)
                        split_here(pe, s)
                        for kk in range(2):
                            k = 2 * kg + kk
                            wh, wl = whl(s, kk, 512)
                            for tb in range(NB):
                                xh, xl = (a[:, k, tb * P:(tb + 1) * P] for a in h)
                                mm(psum[:, 4 + tb, :], xh, wh, k == 0, False)
                                mm(psum[:, 4 + tb, :], xh, wl, False, False)
                                last = mm(psum[:, 4 + tb, :], xl, wh, False, k == KD - 1)
                        last.then_inc(PE, 1)
            token_major("v", "v_read")

            pe.wait_ge(S("v_normed"), NB)
            a = tile_at("mix", 0)
            tile_here(pe, a)
            for hd in range(HG):
                b = block_at("mix", hd)
                block_free(pe, b)
                for n in range(NB):
                    last = mm(psum[:, b.slot, n * P:(n + 1) * P], vtok[:, n, hd * P:(hd + 1) * P],
                              wchunk(a, hd), True, True)
                last.then_inc(PE, 1)
            project("u", HG, 4, h)

            pe.wait_ge(S("yr_ready"), NR)
            pe.wait_ge(S("yg_ready"), HG)

            def merge(u, i):
                for j, (src, kc) in enumerate(((h, KD), (yr, NR), (h, KD), (ygs, KD))):
                    s, b = split_at("merge", 4 * u + j, i, 8), block_at("merge", 4 * u + j, i, 8)
                    split_here(pe, s)
                    block_free(pe, b)
                    for k in range(kc):
                        last = passes(bank(b), s, k, src, k, k == 0, k == kc - 1)
                    last.then_inc(PE, 1)
            rounds(pe, KD, 2, merge)
            project("out", KD, 4, mgs, ready="mg_split")
            norm(1, T)

            def up(half):
                def body(u, i):
                    for j in range(2):
                        s, b = (at(f"up{half}", 2 * u + j, i, 4) for at in (split_at, block_at))
                        split_here(pe, s)
                        block_free(pe, b)
                        for k in range(KD):
                            if not half and isinstance(i, int) and u + i + j == 0:
                                pe.wait_ge(S("norm_done"), KD + k + 1)
                            last = passes(bank(b), s, k, h, k, k == 0, k == KD - 1)
                        last.then_inc(PE, 1)
                rounds(pe, NFH, 2, body)
                project(f"down{half}", KD, 4, ffs, kc=NFH, ready="ff_ready", base=half * NFH)
            up(0)
            up(1)
            norm(2, T)
            norm(3, T)
            project("u2", KS, 4, h, ready="norm_done", base=3 * KD)

            pe.wait_ge(S("u2_ready"), KS)

            def states_in(c):
                pe.wait_ge(S("bw_ready"), c + 1)
                wait(pe, S("bt_ready"), c)
                for k in range(2):
                    last = nc.tensor.transpose(psum[:, 4, k * P:(k + 1) * P], bw[:, c % 2, k * P:(k + 1) * P],
                                               ident[:, :])
                last.then_inc(S("bt_done"), 1)
                pe.wait_ge(S("bt_ready"), c + 1)
                wait(pe, S("xs_read"), 4 * c)
                for k in range(2):
                    last = mm(psum[:, 5 + k, :], bt[:, c % 2, k * P:(k + 1) * P], u2[:, c // 4, :], True, True)
                last.then_inc(S("xs_done"), 1)

            def states_out(c):
                pe.wait_ge(S("s_ready"), 2 * (c + 1))
                if c % 4 == 0:
                    wait(pe, S("ys_read"), c // 4)
                a = tile_at("ssm", c)
                mm(psum[:, 7, :], wchunk(a, 2), ssm_s[:, 2 * (c % 2), :], c % 4 == 0, False)
                mm(psum[:, 7, :], wchunk(a, 3), ssm_s[:, 2 * (c % 2) + 1, :], False, c % 4 == 3).then_inc(PE, 1)
            states_in(0)
            for c in range(NS):
                if c + 1 < NS:
                    states_in(c + 1)
                tile_here(pe, tile_at("ssm", c))
                states_out(c)

            pe.wait_ge(S("ysg_ready"), KS)

            def glu(u, i):
                s = split_at("glu", 2 * u, i, 8)
                split_here(pe, s)
                for j in range(2):
                    b = block_at("glu", 3 * u + j, i, 12)
                    block_free(pe, b)
                    for k in range(KS):
                        last = passes(bank(b), s, 4 * j + k, (ysh, ysl), k, k == 0, k == KS - 1)
                    last.then_inc(PE, 1)
                s, b = split_at("glu", 2 * u + 1, i, 8), block_at("glu", 3 * u + 2, i, 12)
                split_here(pe, s)
                block_free(pe, b)
                for k in range(KD):
                    last = passes(bank(b), s, k, h, k, k == 0, k == KD - 1)
                last.then_inc(PE, 1)
            rounds(pe, KD, 4, glu)

            def head_sum(n):
                pe.wait_ge(S("hsq_ready"), n + 1)
                wait(pe, S("hsd_done"), n - 1)
                mm(psum[:, 4 + n % 2, :], ones[:, :], ht[:, n % 2, :], True, True).then_inc(S("hss_done"), 1)
            for n in range(2 * HEADS):
                stage, hd = ("q", "k")[n // HEADS], n % HEADS
                b, s = block_at(stage, hd), split_at(stage, hd)
                block_free(pe, b)
                split_here(pe, s)
                for k in range(KD):
                    last = passes(bank(b), s, k, h, k, k == 0, k == KD - 1)
                last.then_inc(PE, 1)
                if n:
                    head_sum(n - 1)
            pe.wait_ge(S("hsd_done"), 2 * HEADS - 1)
            token_major("v2", "v2_read")
            a, b = tile_at("f", 0), block_at("f", 0)
            tile_here(pe, a)
            block_free(pe, b)
            for k in range(KD):
                for part in range(2):
                    last = mm(psum[0:HEADS, b.slot, :], wchunk(a, k, HEADS), h[part][:, k, :].bitcast(F32),
                              k + part == 0, k == KD - 1 and part == 1)
            last.then_inc(PE, 1)

            pe.wait_ge(S("v2_read"), 2 * NB)
            head_sum(2 * HEADS - 1)

            pe.wait_ge(S("cum_ready"), 1)
            pe.wait_ge(S("mask_ready"), 2)
            for hd in range(HEADS):
                pe.wait_ge(S("qk_normed"), HEADS + hd + 1)
                for qb in range(NB):
                    b = block_at("attn", 9 * hd + qb)
                    block_free(pe, b)
                    nk = (qb + 1) * P
                    out = bank(b, nk)
                    mm(out, qT[:, hd, qb * P:(qb + 1) * P], kT[:, hd, 0:nk], True, False)
                    mm(out, sel[0:HEADS, hd, :], cumn[:, 0:nk], False, False)
                    mm(psum[:, b.slot, qb * P:nk], ident[:, :], maskt[:, :], False, True).then_inc(PE, 1)
                pe.wait_ge(S("p_ready"), NB * (hd + 1))
                for kb in range(NB):
                    b = block_at("attn", 9 * hd + NB + kb)
                    block_free(pe, b)
                    for qb in range(kb, NB):
                        last = nc.tensor.transpose(psum[:, b.slot, qb * P:(qb + 1) * P],
                                                   probs[:, qb, kb * P:(kb + 1) * P], ident[:, :])
                    last.then_inc(PE, 1)
                b = block_at("attn", 9 * hd + 2 * NB)
                block_free(pe, b)
                for kb in range(NB):
                    pe.wait_ge(S("pt_ready"), NB * hd + kb + 1)
                    last = mm(psum[:, b.slot, kb * P:T], vt2[:, kb, hd * P:(hd + 1) * P],
                              probsT[:, kb, kb * P:T], kb == 0, kb == NB - 1)
                last.then_inc(PE, 1)
            project("ga", KD, 4, h)
            project("out2", KD, 4, mg2s, ready="mg2_split")
            norm(4, T)
            project("query", 16, 4, h, ready="norm_done", base=4 * KD)
            pe.wait_ge(S("pq_ready"), 16)
            for n in range(16):
                a, b = tile_at("keys", n // 8), block_at("keys", n)
                tile_here(pe, a)
                block_free(pe, b)
                for tb in range(NB):
                    last = mm(psum[:, b.slot, tb * P:(tb + 1) * P], pq[:, n, tb * P:(tb + 1) * P],
                              wchunk(a, n % 8), True, True)
                last.then_inc(PE, 1)

            for tb in range(NB):
                pe.wait_ge(S("picks_ready"), tb + 1)
                wait(pe, S("picksT_ready"), tb)
                for k in range(3):
                    last = nc.tensor.transpose(psum[:, 4, k * P:(k + 1) * P], picks[:, tb, k * P:(k + 1) * P],
                                               ident[:, :])
                last.then_inc(S("picksT_done"), 1)

            def spread(u, i):
                b = block_at("gate", u, i, 4)
                block_free(pe, b)
                pe.wait_ge(S("hot_shared"), i * 4 + u + 1)
                for k in range(4):
                    last = mm(psum[:, b.slot, k * P:(k + 1) * P], hot_a[:, u % 4, k * P:(k + 1) * P],
                              hot_b[:, u % 4, k * P:(k + 1) * P], True, True)
                last.then_inc(PE, 1)
            rounds(pe, T // 4, 4, spread)


            def group(i):
                for k in range(JG):
                    s = split_at("experts", k, i, 2 * JG)
                    split_here(pe, s)
                    if k < 4:
                        wait(pe, S("eo_read"), (i - 1) * KD + (k + 5))
                    else:
                        wait(pe, S("ea_ready"), i * JG + (k - 3))
                    for c in range(KD):
                        last = passes(psum[:, 4 + k % 4, :], s, c, h, c, c == 0, c == KD - 1)
                    last.then_inc(PE, 1)
                for half in range(2):
                    if half:
                        pe.wait_ge(S("ea_ready"), i * JG + JG)
                    elif not isinstance(i, int):
                        pe.wait_ge(S("eo_read"), (i - 1) * KD + 4)
                    for m in range(JG // 2):
                        s = split_at("experts", JG + 4 * half + m, i, 2 * JG)
                        split_here(pe, s)
                        for kk in range(2):
                            k = 2 * m + kk
                            if not half:
                                pe.wait_ge(S("ew_ready"), i * JG + (k + 1))
                            for c in range(4):
                                last = passes(psum[:, 4 * half + c, :], s, 4 * kk + c, ews, k, k == 0, k == JG - 1)
                        last.then_inc(PE, 1)
            group(0)
            with pe.Fori(1, PK // JG) as i:
                group(i)

        @block.scalar
        def _(act):
            A = nc.scalar.activation

            act.wait_ge(S("vecs_loaded"), 16)
            A(silu, t3(V("c2"), 2), ACT.Silu).then_inc(S("silu_ready"), 1)
            act.wait_ge(S("sp_abs"), 1)
            A(sp[1], sp[0], ACT.Exp, scale=-1.0).then_inc(S("sp_exp"), 1)
            act.wait_ge(S("sp_one"), 1)
            A(sp[3], sp[2], ACT.Ln).then_inc(S("sp_ln"), 1)
            A(s_step, V("lstep"), ACT.Exp).then_inc(S("s5_act"), 1)
            act.wait_ge(S("s5_dve"), 1)
            A(s_mag, sc[0], ACT.Exp).then_inc(S("s5_act"), 1)
            act.wait_ge(S("s5_dve"), 2)
            A(s_sin, sc[1], ACT.Sin).then_inc(S("s5_act"), 1)
            A(s_cos, sc[2], ACT.Sin).then_inc(S("s5_act"), 1)

            def norm(k, src, cols, ready, first):
                for c in range(KD):
                    act.wait_ge(S(ready), first(c))
                    wait(act, S("sq_used"), k * KD + c - 1)
                    A(nrm[k][c % 2][:, 0:cols], src[:, c, 0:cols], ACT.Square).then_inc(S("sq_ready"), 1)
                act.wait_ge(S("sq_used"), (k + 1) * KD)
                wait(act, S("norm_done"), k * KD)
                sd = nrm[k][2]
                if cols > T:
                    A(sd[:, T:cols], psum[:, 6, 0:cols - T], ACT.Sqrt, scale=1.0 / D, bias=epsc)
                A(sd[:, 0:T], psum[:, 5, :], ACT.Sqrt, scale=1.0 / D, bias=epsc).then_inc(S("sd_done"), 1)
            epsc = V("eps")
            norm(0, xc, TX, "x_loaded", lambda c: 16)

            def rx(u, i):
                n = i * 4 + u
                b0, b1 = block_at("rx", 2 * u, i, 8), block_at("rx", 2 * u + 1, i, 8)
                pad = pads[u % 2]
                wait(act, S("xr_ready"), n - 1)
                block_here(act, b0)
                A(pad[:, 2:2 + T], bank(b0), ACT.Copy).then_inc(S("pad_ready"), 1)
                block_here(act, b1)
                A(pad[:, T + 5:T + 5 + TC], bank(b1, TC), ACT.Copy).then_inc(S("pad_ready"), 1)
            act.wait_ge(S("pads_zero"), 2)
            rounds(act, NR, 4, rx)

            act.wait_ge(S("sp_done"), 1)
            act.wait_ge(S("xr_ready"), NR)
            for n in range(2 * NR):
                j = n % 5
                r_n, i_n = rr[:, n % 2, :], ri[:, n % 2, :]
                wait(act, S("lru_in"), n - 1)
                for g, (dst, bias) in enumerate(((r_n, hba), (i_n, hbx))):
                    for part, (lo, hi) in enumerate(((0, T), (T, TX))):
                        b = block_at(f"gates{n}", 2 * g + part)
                        block_here(act, b)
                        A(dst[:, lo:hi], bank(b, hi - lo), ACT.Tanh, scale=0.5, bias=bias[:, n:n + 1])\
                            .then_inc(S("gate_tanh"), 1)
                wait(act, S("lru_done"), 5 * (n // 5))
                act.wait_ge(S("gate_tanh"), 4 * n + 2)
                A(lw[:, j, :], r_n, ACT.Tanh, scale=sp2[:, n:n + 1], bias=sp2[:, n:n + 1]).then_inc(S("decay"), 1)
                A(la[:, j, :], r_n, ACT.Exp, scale=sp4n[:, n:n + 1], bias=sp4n[:, n:n + 1]).then_inc(S("decay"), 1)
                if j == 4:
                    for k in range(5):
                        act.wait_ge(S("a_ready"), n - 4 + k + 1)
                        A(lw[:, k, :], lw[:, k, :], ACT.Sqrt).then_inc(S("root"), 1)

            act.wait_ge(S("lru_done"), 2 * NR)

            def gelu_into(stage, sem, used):
                def body(u, i):
                    n = i * 4 + u
                    b = block_at(stage, u, i, 4)
                    block_here(act, b)
                    wait(act, S(used), n - 1)
                    A(gt[:, u % 2, :], bank(b), ACT.Gelu_apprx_tanh).then_inc(S(sem), 1)
                return body
            rounds(act, NR, 4, gelu_into("rg", "rg_gelu", "yr_ready"))

            for half in range(2):
                tile_used(act, tile_at("v", 4 * half + 3))
                for tb in range(NB):
                    A(vtok[:, tb, half * 512:(half + 1) * 512], psum[:, 4 + tb, :], ACT.Gelu_apprx_tanh)\
                        .then_inc(S("v_read"), 1)
            act.wait_ge(S("v_read"), 2 * NB)
            for tb in range(NB):
                if tb:
                    act.wait_ge(S("v_sq"), tb)
                A(vjunk, vtok[:, tb, :], ACT.Square, accum_out=vss[:, tb:tb + 1])\
                    .then_inc(S("v_sq"), 1)
            act.wait_ge(S("v_sq"), NB)
            A(vsd, vss, ACT.Sqrt, scale=1.0 / W_G, bias=epsc).then_inc(S("v_sd"), 1)
            act.wait_ge(S("yr_ready"), NR)
            rounds(act, HG, 4, gelu_into("u", "u_gelu", "yg_ready"))
            act.wait_ge(S("yg_ready"), HG)

            def merge(u, i):
                for j in range(2):
                    b = block_at("merge", 4 * u + 2 * j, i, 8)
                    block_here(act, b)
                    wait(act, S("merged"), i * 2 + (u - 1))
                    A(mt[:, 2 * (u % 2) + j, :], bank(b), ACT.Tanh, scale=0.5).then_inc(S("merge_tanh"), 1)
            rounds(act, KD, 2, merge)
            norm(1, x, T, "x_mixed", lambda c: c + 1)

            act.wait_ge(S("ffpads_zero"), 2)

            def up(half):
                def body(units, i):
                    for u in units:
                        n = i * 2 + (u + half * NFH)
                        b = block_at(f"up{half}", 2 * u, i, 4)
                        f = (u + half * NFH) % 2
                        wait(act, S("ffconv"), (n - 1) * 9)
                        block_here(act, b)
                        A(ffp[f][:, 1:1 + GH, 1:1 + GW], bank(b).rearrange("p (r c) -> p r c", c=GW), ACT.Copy)\
                            .then_inc(S("ffpad_ready"), 1)
                    for u in units:
                        n = i * 2 + (u + half * NFH)
                        f = (u + half * NFH) % 2
                        act.wait_ge(S("ffconv"), (n + 1) * 9)
                        wait(act, S("ff_used"), n - 1)
                        A(fge[:, f, :], fcv[:, f, :], ACT.Gelu_apprx_tanh).then_inc(S("ff_gelu"), 1)
                grouped(act, NFH, 2, body)
            up(0)
            up(1)
            norm(2, x, T, "x_ffn", lambda c: KD + c + 1)
            norm(3, x, T, "norm_done", lambda c: 2 * KD + c + 1)

            def copy_out(stage, dst, sem, per=4):
                def body(u, i):
                    b = block_at(stage, u, i, per)
                    block_here(act, b)
                    A(pick(dst, i * per + u), bank(b), ACT.Copy).then_inc(S(sem), 1)
                return body
            rounds(act, KS, 4, copy_out("u2", u2, "u2_ready"))

            for c in range(NS):
                act.wait_ge(S("bt_done"), c + 1)
                wait(act, S("xs_done"), c - 1)
                A(bt[:, c % 2, :], psum[:, 4, 0:2 * P], ACT.Copy).then_inc(S("bt_ready"), 1)
                if c % 4 == 1 and c > 1:
                    act.wait_ge(S("ys_read"), c // 4)
                    A(ysk, ysk, ACT.Gelu_apprx_tanh).then_inc(S("ys_gelu"), 1)
            act.wait_ge(S("ys_read"), KS)
            A(ysk, ysk, ACT.Gelu_apprx_tanh).then_inc(S("ys_gelu"), 1)

            def glu(u, i):
                for j in range(2):
                    b = block_at("glu", 3 * u + 1 + j, i, 12)
                    block_here(act, b)
                    wait(act, S("glu_done"), i * 4 + (u - 1))
                    A(gl[:, 2 * (u % 2) + j, :], bank(b), ACT.Tanh, scale=0.5).then_inc(S("glu_tanh"), 1)
            rounds(act, KD, 4, glu)

            def head_root(n):
                act.wait_ge(S("hss_done"), n + 1)
                wait(act, S("qk_normed"), n - 1)
                A(ht[:, 2 + n % 2, :], psum[:, 4 + n % 2, :], ACT.Sqrt, scale=1.0 / P, bias=epsc)\
                    .then_inc(S("hsd_done"), 1)
            for n in range(2 * HEADS):
                name, dst, hd = ("q", "k")[n // HEADS], (qT, kT)[n // HEADS], n % HEADS
                copy_out(name, dst, f"{name}_ready")(hd % 4, hd // 4)
                act.wait_ge(S(f"{name}_ready"), hd + 1)
                wait(act, S("hss_done"), n - 1)
                A(ht[:, n % 2, :], dst[:, hd, :], ACT.Square).then_inc(S("hsq_ready"), 1)
                if n:
                    head_root(n - 1)
            for half in range(2):
                tile_used(act, tile_at("v2", 4 * half + 3))
                for tb in range(NB):
                    A(vt2[:, tb, half * 512:(half + 1) * 512], psum[:, 4 + tb, :], ACT.Copy).then_inc(S("v2_read"), 1)
            act.wait_ge(S("f_abs"), 1)
            A(fl[1], fl[2], ACT.Exp, scale=-1.0).then_inc(S("f_act"), 1)
            act.wait_ge(S("f_one"), 1)
            A(fl[4], fl[3], ACT.Ln).then_inc(S("f_act"), 1)

            head_root(2 * HEADS - 1)

            act.wait_ge(S("qk_normed"), 2 * HEADS)
            for hd in range(HEADS):
                for qb in range(NB):
                    at = NB * (hd % 2) + qb
                    act.wait_ge(S("amax"), NB * hd + qb + 1)
                    if hd:
                        block_here(act, block_at("attn", 9 * (hd - 1) + 2 * NB - 1))
                    A(probs[:, qb, 0:(qb + 1) * P], bank(block_at("attn", 9 * hd + qb), (qb + 1) * P), ACT.Exp,
                      bias=nmx[:, at:at + 1], accum_out=rs[:, at:at + 1]).then_inc(S("p_exp"), 1)
                b = block_at("attn", 9 * hd + 2 * NB)
                block_here(act, b)
                A(qT[:, hd, :], bank(b), ACT.Copy).then_inc(S("o_ready"), 1)

            def ga(u, i):
                b = block_at("ga", u, i, 4)
                block_here(act, b)
                wait(act, S("ga_mul"), i * 4 + (u - 1))
                A(gat[:, u % 2, :], bank(b), ACT.Tanh, scale=0.5).then_inc(S("ga_tanh"), 1)
            rounds(act, KD, 4, ga)
            norm(4, x, T, "x_mixed2", lambda c: c + 1)
            rounds(act, 16, 4, copy_out("query", pq, "pq_ready"))
            for n in range(16):
                b = block_at("keys", n)
                block_here(act, b)
                wait(act, S("topk_done"), n - 3)
                A(scb[:, n % 4, :], bank(b), ACT.Copy).then_inc(S("sc_ready"), 1)
            for tb in range(NB):
                act.wait_ge(S("best_ready"), tb + 1)
                A(bexp, fa, ACT.Exp).then_inc(S("best_exp"), 1)
                act.wait_ge(S("picksT_done"), tb + 1)
                A(picksT[:, :, tb * P:(tb + 1) * P], t3(psum[:, 4, 0:3 * P], P), ACT.Copy)\
                    .then_inc(S("picksT_ready"), 1)

            def spread(u, i):
                n = i * 32 + u
                if u % 16 == 0:
                    wait(act, S(f"gates_parked{u // 16}"), i * 16)
                b = block_at("gate", u, i, 32)
                block_here(act, b)
                t0 = 4 * (u % 16)
                A(stage[u // 16][:, :, t0:t0 + 4].rearrange("p j t -> p t j"), t3(bank(b), P), ACT.Copy)\
                    .then_inc(S("gates_staged"), 1)
            act.wait_ge(S("picksT_ready"), NB)
            rounds(act, T // 4, 32, spread)

            def group(i):
                for k in range(JG):
                    tile_used(act, tile_at("experts", k, i, 2 * JG))
                    wait(act, S("ew_raw"), i * JG + (k - 3))
                    A(ga4[:, k % 4, :], psum[:, 4 + k % 4, :], ACT.Gelu_apprx_tanh).then_inc(S("ea_ready"), 1)
            group(0)
            with act.Fori(1, PK // JG) as i:
                group(i)

        @block.vector
        def _(ve):
            v = nc.vector
            link = chain(ve, S("dve_step"))
            TT, TS, STT = v.tensor_tensor, v.tensor_scalar, v.scalar_tensor_tensor

            for k in range(2):
                v.memset(pads[k], 0.0).then_inc(S("pads_zero"), 1)
            ve.wait_ge(S("vecs_loaded"), 16)

            def split(step, dst, n, src):
                hi, lo = pick(dst[0], n), pick(dst[1], n)
                step(v.tensor_copy(hi, src))
                return TT(lo, src, hi.bitcast(F32), ALU.subtract)

            def log1p_exp(absx, e, one, ln, d, w):
                link(TS(d, one, -1.0, None, ALU.add))
                link(TS(w, d, 2.0 ** -40, None, ALU.max))
                link(v.reciprocal(w, w))
                link(TT(w, w, ln, ALU.mult))
                link(TT(w, w, e, ALU.mult))
                link(STT(d, d, 0.0, e, ALU.is_equal, ALU.mult))
                link(TT(w, w, d, ALU.add))

            link(STT(sp[0], V("lam"), -1.0, V("lam"), ALU.mult, ALU.max))
            ve.sem_inc(S("sp_abs"), 1)
            ve.wait_ge(S("sp_exp"), 1)
            link(TS(sp[2], sp[1], 1.0, None, ALU.add))
            ve.sem_inc(S("sp_one"), 1)
            ve.wait_ge(S("sp_ln"), 1)
            log1p_exp(sp[0], sp[1], sp[2], sp[3], sp[4], sp[5])
            link(TS(sp[4], V("lam"), -1.0, 0.0, ALU.mult, ALU.max))
            link(TT(sp[5], sp[5], sp[4], ALU.add))
            link(TS(sp2, sp[5], 2.0, None, ALU.mult))
            link(TS(sp4n, sp[5], -4.0, None, ALU.mult))
            link(TS(hba, V("ba"), 0.5, None, ALU.mult))
            link(TS(hbx, V("bx"), 0.5, None, ALU.mult))
            ve.sem_inc(S("sp_done"), 1)

            ar, ai = V("are"), V("aim")
            ve.wait_ge(S("s5_act"), 1)
            link(TT(sc[0], ar, s_step, ALU.mult))
            link(TT(sc[3], ai, s_step, ALU.mult))
            ve.sem_inc(S("s5_dve"), 1)
            link(TS(sc[4], sc[3], 1.0 / TWO_PI, ROUND, ALU.mult, ALU.add))
            link(TS(sc[4], sc[4], -ROUND, None, ALU.add))
            for part in TWO_PI_PARTS:
                link(STT(sc[3], sc[4], -part, sc[3], ALU.mult, ALU.add))
            link(TS(sc[1], sc[3], PI_LESS, -PI_LESS, ALU.min, ALU.max))
            link(STT(sc[2], sc[1], -1.0, sc[1], ALU.mult, ALU.max))
            link(TS(sc[2], sc[2], -1.0, math.pi / 2, ALU.mult, ALU.add))
            ve.sem_inc(S("s5_dve"), 1)
            ve.wait_ge(S("s5_act"), 4)
            link(TT(sc[5], s_mag, s_cos, ALU.mult))
            link(TS(sc[5], sc[5], -1.0, None, ALU.add))
            link(TT(sc[6], s_mag, s_sin, ALU.mult))
            link(TT(sc[7], ar, ar, ALU.mult))
            link(TT(sc[8], ai, ai, ALU.mult))
            link(TT(sc[7], sc[7], sc[8], ALU.add))
            link(v.reciprocal(sc[7], sc[7]))
            for out, (p, q, op) in ((cr, (sc[5], sc[6], ALU.add)), (ci, (sc[6], sc[5], ALU.subtract))):
                link(TT(sc[8], p, ar, ALU.mult))
                link(TT(sc[9], q, ai, ALU.mult))
                link(TT(sc[8], sc[8], sc[9], op))
                link(TT(out, sc[8], sc[7], ALU.mult))
            link(v.tensor_copy(pw[:, 0, 0, :], s_cos))
            link(v.tensor_copy(pw[:, 0, 1, :], s_sin))
            for k in range(8):
                c0, s0 = pw[:, k, 0, :], pw[:, k, 1, :]
                link(TT(sc[8], c0, c0, ALU.mult))
                link(TT(sc[9], s0, s0, ALU.mult))
                link(TT(pw[:, k + 1, 0, :], sc[8], sc[9], ALU.subtract))
                link(STT(pw[:, k + 1, 1, :], c0, 2.0, s0, ALU.mult, ALU.mult))

            def angles(table, k):
                cos, sin, work, first, n = table
                w = 2 ** k
                if k == 0:
                    link(v.memset(cos[:, :, 0:1], 1.0))
                    link(v.memset(sin[:, :, 0:1], 0.0))
                pc, ps = (pw[:, k, j, first:first + n].unsqueeze(2).to_broadcast([P, n, w]) for j in range(2))
                c0, s0, c1, s1 = cos[:, :, 0:w], sin[:, :, 0:w], cos[:, :, w:2 * w], sin[:, :, w:2 * w]
                tmp = work.rearrange("p c w -> p (c w)")[:, 0:n * w].rearrange("p (c w) -> p c w", w=w)
                link(TT(c1, c0, pc, ALU.mult))
                link(TT(tmp, s0, ps, ALU.mult))
                link(TT(c1, c1, tmp, ALU.subtract))
                link(TT(s1, s0, pc, ALU.mult))
                link(TT(tmp, c0, ps, ALU.mult))
                link(TT(s1, s1, tmp, ALU.add))

            ve.wait_ge(S("sd_done"), 1)
            link(v.reciprocal(nrm[0][3], nrm[0][2]))
            for c in range(KD):
                TT(xc[:, c, :], xc[:, c, :], nrm[0][3], ALU.mult).then_inc(S("xc_divided"), 1)
            ve.wait_ge(S("xc_divided"), KD)

            bm = V("bmod").unsqueeze(2).to_broadcast([P, 48, 2])
            pm = psum[:, 4, 0:96].rearrange("p (n k) -> p n k", k=2)
            tile_used(ve, tile_at("moda", 15))
            TT(mod[:, 0:16, :], pm[:, 0:16, :], bm[:, 0:16, :], ALU.add).then_inc(S("mod_read"), 1)
            ve.wait_ge(S("mod_read"), 1)
            for k in range(2):
                link(STT(a1[:, :, k], mod[:, 8:16, k], 1.0, V("g1"), ALU.add, ALU.mult))

            def norm(k, src, cols, scale, shift, dst=None):
                sd, rstd = nrm[k][2], nrm[k][3]
                if cols == T:
                    ve.wait_ge(S("sd_done"), k + 1)
                    link(v.reciprocal(rstd, sd))
                for c in range(KD):
                    if cols > T:
                        raw = src[:, c, :]
                    else:
                        raw = dst[:, c, :] if dst is not None else nrm[k][4 + c % 2]
                        link(TT(raw, src[:, c, :], rstd, ALU.mult))
                    for kk, (lo, hi, out) in enumerate(((0, T, h), (T, cols, hc)) if cols > T else ((0, T, h),)):
                        r = raw[:, lo:hi]
                        if cols > T:
                            ins = TS(r, r, scale[:, c, kk:kk + 1], shift[:, c, kk:kk + 1], ALU.mult, ALU.add)
                        elif shift is None:
                            ins = TS(r, r, scale[:, c:c + 1], None, ALU.mult)
                        else:
                            ins = TS(r, r, scale[:, c:c + 1], shift[:, c, 0:1], ALU.mult, ALU.add)
                        if dst is None:
                            link(ins)
                            ins = split(link, out, c, r)
                        if hi < cols:
                            link(ins)
                    ins.then_inc(S("norm_done"), 1)
                    if c >= KD - 2 or dst is None:
                        ve.wait_ge(S("norm_done"), k * KD + c + 1)
            norm(0, xc, TX, a1, mod[:, 0:8, :])

            def rx(u, i):
                n = i * 4 + u
                pad = pads[u % 2]
                step = chain(ve, S("conv_step"), n * 7)
                ve.wait_ge(S("pad_ready"), n * 2 + 2)
                for j, (at, lo, w) in enumerate(((0, 0, T), (T + 3, T, TC))):
                    out = pick(xr, n)[:, lo:lo + w]
                    step(TS(out, pad[:, at:at + w], tap(n, 0), col(V("convb"), n), ALU.mult, ALU.add))
                    for k in range(1, KR):
                        ins = STT(out, pad[:, at + k:at + k + w], tap(n, k), out, ALU.mult, ALU.add)
                        if j == 1 and k == KR - 1:
                            ins.then_inc(S("xr_ready"), 1)
                        else:
                            step(ins)

            def tap(n, k):
                return col(V("convw"), n * KR + k)
            ve.wait_ge(S("pads_zero"), 2)
            rounds(ve, NR, 4, rx)

            def scan_group(g):
                for j in range(5):
                    n = 5 * g + j
                    c = n % NR
                    ve.wait_ge(S("decay"), 2 * n + 2)
                    link(STT(lq, la[:, j, :], 1.0, lw[:, j, :], ALU.add, ALU.mult))
                    TS(la[:, j, :], lq, -1.0, 1.0, ALU.mult, ALU.add).then_inc(S("a_ready"), 1)
                    ve.wait_ge(S("gate_tanh"), 4 * n + 4)
                    STT(lb[:, j, :], ri[:, n % 2, :], 1.0, xr[:, c, :], ALU.add, ALU.mult).then_inc(S("lru_in"), 1)
                    ve.wait_ge(S("lru_in"), n + 1)
                    link(STT(lb[:, j, :], la[:, j, :], 1.0, lb[:, j, :], ALU.add, ALU.mult))
                for j in range(5):
                    n = 5 * g + j
                    c = n % NR
                    ve.wait_ge(S("root"), n + 1)
                    link(STT(lb[:, j, :], lb[:, j, :], 0.5, lw[:, j, :], ALU.mult, ALU.mult))
                    aj, bj = la[:, j, :], lb[:, j, :]
                    if n < NR:
                        link(v.tensor_tensor_scan(cs, aj[:, T:TX], bj[:, T:TX], 0.0, ALU.mult, ALU.add))
                        v.tensor_tensor_scan(y[:, c, :], aj[:, 0:T], bj[:, 0:T], cs[:, TC - 1:TC], ALU.mult,
                                             ALU.add).then_inc(S("lru_done"), 1)
                    else:
                        link(v.tensor_tensor_scan(cs[:, ::-1], aj[:, T:TX][:, ::-1], bj[:, T:TX][:, ::-1], 0.0,
                                                  ALU.mult, ALU.add))
                        link(v.tensor_tensor_scan(yb[:, ::-1], aj[:, 0:T][:, ::-1], bj[:, 0:T][:, ::-1],
                                                  cs[:, 0:1], ALU.mult, ALU.add))
                        TT(y[:, c, :], y[:, c, :], yb, ALU.add).then_inc(S("lru_done"), 1)
            ve.wait_ge(S("norm_done"), KD)
            ve.wait_ge(S("xr_ready"), NR)
            for g in range(4):
                scan_group(g)
            ve.wait_ge(S("lru_done"), 2 * NR)

            def times_gelu(src, dst, sem, ready, work):
                def body(u, i):
                    n = i * 4 + u
                    step = chain(ve, S(work), n * 2)
                    ve.wait_ge(S(sem), n + 1)
                    step(TT(pick(src, n), pick(src, n), gt[:, u % 2, :], ALU.mult))
                    split(step, dst, n, pick(src, n)).then_inc(S(ready), 1)
                return body
            rounds(ve, NR, 4, times_gelu(y, yr, "rg_gelu", "yr_ready", "yr_step"))

            tile_used(ve, tile_at(f"modb{2 * NR - 1}", MODB[-1] - MODB[-2] - 1))
            TT(mod[:, 16:48, :], pm[:, 16:48, :], bm[:, 16:48, :], ALU.add).then_inc(S("mod_read"), 1)
            ve.wait_ge(S("mod_read"), 2)
            link(TS(hm2, mod[:, 16:24, 0], 0.5, None, ALU.mult))
            link(STT(a2, mod[:, 32:40, 0], 1.0, V("g2"), ALU.add, ALU.mult))

            ve.wait_ge(S("v_sd"), 1)
            link(v.reciprocal(vrs, vsd))
            for tb in range(NB):
                TS(vtok[:, tb, :], vtok[:, tb, :], vrs[:, tb:tb + 1], None, ALU.mult).then_inc(S("v_normed"), 1)
            ve.wait_ge(S("bsrow_loaded"), 16)
            for hd in range(HG):
                b = block_at("mix", hd)
                block_here(ve, b)
                STT(t3(yg[:, hd, :], P), t3(bank(b), P), V("gv")[:, hd:hd + 1],
                    bsrow[:, hd:hd + 1, :].to_broadcast([P, NB, P]), ALU.mult, ALU.add)\
                    .then_inc(S("yg_mixed"), 1)
            ve.wait_ge(S("yg_mixed"), HG)
            rounds(ve, HG, 4, times_gelu(yg, ygs, "u_gelu", "yg_ready", "yg_step"))

            def merge(u, i):
                n = i * 2 + u
                for j in range(2):
                    b = block_at("merge", 4 * u + 2 * j + 1, i, 8)
                    block_here(ve, b)
                    ve.wait_ge(S("merge_tanh"), n * 2 + (j + 1))
                    STT(mt[:, 2 * (u % 2) + j, :], mt[:, 2 * (u % 2) + j, :], 1.0, bank(b), ALU.add, ALU.mult)\
                        .then_inc(S("merge_mul"), 1)
                ve.wait_ge(S("merge_mul"), n * 2 + 2)
                TT(pick(mg, n), mt[:, 2 * (u % 2), :], mt[:, 2 * (u % 2) + 1, :], ALU.add).then_inc(S("merged"), 1)
            rounds(ve, KD, 2, merge)

            def add_to_x(stage, sem, scale):
                def body(u, i):
                    n = i * 4 + u
                    b = block_at(stage, u, i, 4)
                    block_here(ve, b)
                    STT(pick(x, n), bank(b), scale(n), pick(x, n), ALU.mult, ALU.add).then_inc(S(sem), 1)
                return body
            ve.wait_ge(S("merged"), KD)
            for n in range(KD):
                split(link, mgs, n, mg[:, n, :]).then_inc(S("mg_split"), 1)
            ve.wait_ge(S("xres_loaded"), 16)
            rounds(ve, KD, 4, add_to_x("out", "x_mixed", lambda n: col(hm2, n)))
            ve.wait_ge(S("x_mixed"), KD)
            for k in range(2):
                v.memset(ffp[k], 0.0).then_inc(S("ffpads_zero"), 1)
            norm(1, x, T, a2, mod[:, 24:32, :])

            def up(half):
                def body(units, i):
                    for u in units:
                        n = i * 2 + (u + half * NFH)
                        f = (u + half * NFH) % 2
                        cv = fcv[:, f, :].rearrange("p (r c) -> p r c", c=GW)
                        step = chain(ve, S("ffconv"), n * 9)
                        ve.wait_ge(S("ffpad_ready"), n + 1)
                        wait(ve, S("ff_gelu"), n - 1)
                        for t in range(9):
                            win = ffp[f][:, t // 3:t // 3 + GH, t % 3:t % 3 + GW]
                            w = col(V("fcw"), n * 9 + t)
                            if t == 0:
                                step(TS(cv, win, w, col(V("fcb"), n), ALU.mult, ALU.add))
                            else:
                                step(STT(cv, win, w, cv, ALU.mult, ALU.add))
                    for u in units:
                        n = i * 2 + (u + half * NFH)
                        f = (u + half * NFH) % 2
                        b = block_at(f"up{half}", 2 * u + 1, i, 4)
                        block_here(ve, b)
                        ve.wait_ge(S("ff_gelu"), n + 1)
                        wait(ve, S("ff_ready"), n - 1)
                        TT(fra[:, f, :], fge[:, f, :], bank(b), ALU.mult).then_inc(S("ff_used"), 1)
                        ve.wait_ge(S("ff_used"), n + 1)
                        split(chain(ve, S("ff_step"), n), ffs, i * 2 + u, fra[:, f, :]).then_inc(S("ff_ready"), 1)
                if half:
                    ve.wait_ge(S("pe_done"), USED[TILE0["down0"] + KD - 1])
                grouped(ve, NFH, 2, body)
                add = add_to_x(f"down{half}", "x_ffn", lambda n: mod_t[:, 2 * n + 80:2 * n + 81] if isinstance(n, int)
                               else mod_t[:, bass.ds(n * 2 + 80, 1)])
                if half:
                    for n in range(KD):
                        add(n % 4, n // 4)
                        for k in ((0, 1, 2, 3, 4), (5,), (6,), (7,), (8,))[n] if n < 5 else ():
                            angles(tables[0], k)
                else:
                    rounds(ve, KD, 4, add)
                ve.wait_ge(S("x_ffn"), KD * (half + 1))
            ve.wait_ge(S("ffpads_zero"), 2)
            up(0)
            up(1)
            norm(2, x, T, V("gfin"), None, dst=x)
            norm(3, x, T, V("mixg"), None)
            for k in range(9):
                angles(tables[1], k)

            def input_map(c):
                a = tile_at("ssm", c)
                tile_here(ve, a)
                bre, bim = wchunk(a, 0), wchunk(a, 1)
                wait(ve, S("bt_done"), c - 1)
                wait(ve, S("bw_ready"), c)
                TS(bt1, bim, ci[:, c:c + 1], None, ALU.mult).then_inc(S("map_step"), 1)
                TS(bt2, bre, ci[:, c:c + 1], None, ALU.mult).then_inc(S("map_step"), 1)
                ve.wait_ge(S("map_step"), 2 * c + 1)
                STT(bw[:, c % 2, 0:P], bre, cr[:, c:c + 1], bt1, ALU.mult, ALU.subtract)
                ve.wait_ge(S("map_step"), 2 * c + 2)
                STT(bw[:, c % 2, P:2 * P], bim, cr[:, c:c + 1], bt2, ALU.mult, ALU.add).then_inc(S("bw_ready"), 1)

            def halve(oc):
                ve.wait_ge(S("ys_gelu"), oc + 1)
                split(link, (ysh, ysl), oc, ysk).then_inc(S("ysg_ready"), 1)
                ve.wait_ge(S("ysg_ready"), oc + 1)

            input_map(0)
            for c in range(NS):
                if c + 1 < NS:
                    input_map(c + 1)
                cc, ss = (tables[c // 12][k][:, c % 12, :] for k in range(2))
                ve.wait_ge(S("xs_done"), c + 1)
                wait(ve, S("turned"), 2 * c)
                for k, (bk, tab) in enumerate(((5, cc), (6, ss), (6, cc), (5, ss))):
                    TT(st[:, k, :], psum[:, bk, :], tab, ALU.mult).then_inc(S("xs_read"), 1)
                mag = s_mag[:, c:c + 1].to_broadcast([P, T])
                step = S("scan_step")
                for k, op in enumerate((ALU.add, ALU.subtract)):
                    ve.wait_ge(S("xs_read"), 4 * c + 2 * k + 2)
                    TT(st[:, 2 * k, :], st[:, 2 * k, :], st[:, 2 * k + 1, :], op).then_inc(step, 1)
                for k in range(2):
                    ve.wait_ge(step, 4 * c + k + 1)
                    v.tensor_tensor_scan(st[:, 2 * k + 1, :], mag, st[:, 2 * k, :], 0.0, ALU.mult, ALU.add)\
                        .then_inc(step, 1)
                wait(ve, S("s_ready"), 2 * c)
                ve.wait_ge(step, 4 * c + 3)
                TT(st[:, 4, :], st[:, 1, :], cc, ALU.mult)
                ve.wait_ge(step, 4 * c + 4)
                TT(st[:, 5, :], st[:, 3, :], ss, ALU.mult).then_inc(S("turned"), 1)
                TT(back[:, 0, :], st[:, 1, :], ss, ALU.mult)
                STT(back[:, 1, :], st[:, 3, :], -1.0, cc, ALU.mult, ALU.mult).then_inc(S("turned"), 1)
                if c % 4 == 0 and c:
                    skip(ve, c // 4 - 1)
                if c % 4 == 1 and c > 1:
                    halve(c // 4 - 1)
            skip(ve, KS - 1)
            halve(KS - 1)

            def glu(u, i):
                n = i * 4 + u
                b = block_at("glu", 3 * u, i, 12)
                block_here(ve, b)
                ve.wait_ge(S("glu_tanh"), n * 2 + 1)
                wait(ve, S("glu_done"), n - 1)
                STT(gl[:, 4 + u % 2, :], gl[:, 2 * (u % 2), :], 1.0, bank(b), ALU.add, ALU.mult)\
                    .then_inc(S("glu_mul"), 1)
                ve.wait_ge(S("glu_mul"), n + 1)
                ve.wait_ge(S("glu_tanh"), n * 2 + 2)
                STT(pick(mg2, n), gl[:, 2 * (u % 2) + 1, :], 1.0, gl[:, 4 + u % 2, :], ALU.add, ALU.mult)\
                    .then_inc(S("glu_done"), 1)
            rounds(ve, KD, 4, glu)

            ve.wait_ge(S("glu_done"), KD)
            link(TS(dcol[:, 0:1], V("qg"), HEAD_SCALE, None, ALU.mult))

            def head_norm(n):
                dst = (qT if n < HEADS else kT)[:, n % HEADS, :]
                g = dcol[:, 0:1] if n < HEADS else V("kg")
                ve.wait_ge(S("hsd_done"), n + 1)
                wait(ve, S("qk_normed"), n - 1)
                link(v.reciprocal(ht[:, 4 + n % 2, :], ht[:, 2 + n % 2, :]))
                ve.wait_ge(S("hss_done"), n + 1)
                STT(dst, dst, g, ht[:, 4 + n % 2, :], ALU.mult, ALU.mult).then_inc(S("qk_normed"), 1)
            for n in range(2 * HEADS - 1):
                head_norm(n)

            b = block_at("f", 0)
            block_here(ve, b)
            TS(fl[0], psum[0:HEADS, b.slot, :], V("fbias")[0:HEADS, :], None, ALU.add).then_inc(S("f_read"), 1)
            ve.wait_ge(S("f_read"), 1)
            STT(fl[2], fl[0], -1.0, fl[0], ALU.mult, ALU.max).then_inc(S("f_abs"), 1)
            ve.wait_ge(S("f_act"), 1)
            TS(fl[3], fl[1], 1.0, None, ALU.add).then_inc(S("f_one"), 1)
            ve.wait_ge(S("f_one"), 1)
            ve.wait_ge(S("f_act"), 2)
            log1p_exp(fl[2], fl[1], fl[3], fl[4], fl[5], fl[6])
            link(TS(fl[5], fl[0], 0.0, -1.0, ALU.min, ALU.mult))
            link(TT(fl[6], fl[6], fl[5], ALU.add))
            link(v.memset(fl[7], 1.0))
            v.tensor_tensor_scan(cumn, fl[7], fl[6], 0.0, ALU.mult, ALU.add).then_inc(S("cum_ready"), 1)

            head_norm(2 * HEADS - 1)

            for hd in range(HEADS):
                at = NB * (hd % 2)
                for qb in range(NB):
                    b = block_at("attn", 9 * hd + qb)
                    block_here(ve, b)
                    v.tensor_reduce(nmx[:, at + qb:at + qb + 1], bank(b, (qb + 1) * P), AX, ALU.max, negate=True)\
                        .then_inc(S("amax"), 1)
                for qb in range(NB):
                    ve.wait_ge(S("p_exp"), NB * hd + qb + 1)
                    link(v.reciprocal(rrs[:, at + qb:at + qb + 1], rs[:, at + qb:at + qb + 1]))
                    TS(probs[:, qb, 0:(qb + 1) * P], probs[:, qb, 0:(qb + 1) * P], rrs[:, at + qb:at + qb + 1], None,
                       ALU.mult).then_inc(S("p_ready"), 1)
                if hd:
                    block_here(ve, block_at("attn", 9 * (hd - 1) + 2 * NB))
                for kb in range(NB):
                    b = block_at("attn", 9 * hd + NB + kb)
                    block_here(ve, b)
                    v.tensor_copy(probsT[:, kb, kb * P:T], psum[:, b.slot, kb * P:T]).then_inc(S("pt_ready"), 1)

            def ga(u, i):
                n = i * 4 + u
                ve.wait_ge(S("ga_tanh"), n + 1)
                wait(ve, S("merged2"), n - 1)
                STT(gat[:, 2 + u % 2, :], gat[:, u % 2, :], 1.0, pick(qT, n), ALU.add, ALU.mult)\
                    .then_inc(S("ga_mul"), 1)
                ve.wait_ge(S("ga_mul"), n + 1)
                STT(pick(mg2, n), pick(mg2, n), 0.5, gat[:, 2 + u % 2, :], ALU.mult, ALU.add)\
                    .then_inc(S("merged2"), 1)
                ve.wait_ge(S("merged2"), n + 1)
                split(chain(ve, S("mg2_step"), n), mg2s, n, pick(mg2, n)).then_inc(S("mg2_split"), 1)
            ve.wait_ge(S("o_ready"), HEADS)
            rounds(ve, KD, 4, ga)
            rounds(ve, KD, 4, add_to_x("out2", "x_mixed2", lambda n: 0.5))
            ve.wait_ge(S("x_mixed2"), KD)
            norm(4, x, T, V("ffng"), None)

            lane_base = [0]

            def top16(vals, idx, src, w):
                go = lanes(ve, S("lane_step"), 4, lane_base[0])
                for j in range(4):
                    go(v.max(vals[j][:, 0:8], src[j]))
                for j in range(4):
                    go(v.max_index(idx[j][:, 0:8], vals[j][:, 0:8], src[j]))
                for j in range(4):
                    go(v.match_replace(spare[:, j, 0:w], vals[j][:, 0:8], src[j], NEG))
                for j in range(4):
                    go(v.max(vals[j][:, 8:16], spare[:, j, 0:w]))
                for j in range(4):
                    go(v.max_index(idx[j][:, 8:16], vals[j][:, 8:16], spare[:, j, 0:w]))
                lane_base[0] += 20
                ve.wait_ge(S("lane_step"), lane_base[0])
            for n in range(16):
                ve.wait_ge(S("sc_ready"), n + 1)
                at = n * TOPK
                top16([tops[:, tb, at:at + TOPK] for tb in range(NB)],
                      [topi[:, tb, at:at + TOPK].bitcast(U32) for tb in range(NB)],
                      [scb[:, n % 4, tb * P:(tb + 1) * P] for tb in range(NB)], P)
                ve.sem_inc(S("topk_done"), 1)
            for tb in range(NB):
                v.tensor_copy(topf[:, tb, :], topi[:, tb, :].bitcast(U32)).then_inc(S("topf_ready"), 1)
            ve.wait_ge(S("topf_ready"), NB)
            for tb in range(NB):
                for h0 in range(0, PH, 4):
                    for j in range(4):
                        s0 = tops[:, tb, 2 * (h0 + j) * TOPK:(2 * (h0 + j) + 1) * TOPK]
                        s1 = tops[:, tb, (2 * (h0 + j) + 1) * TOPK:(2 * (h0 + j) + 2) * TOPK]
                        TT(t3(cand[:, j, :], TOPK), s0.unsqueeze(2).to_broadcast([P, TOPK, TOPK]),
                           s1.unsqueeze(1).to_broadcast([P, TOPK, TOPK]), ALU.add).then_inc(S("cand_ready"), 1)
                    ve.wait_ge(S("cand_ready"), PH * tb + h0 + 4)
                    rows = [slice((h0 + j) * TOPK, (h0 + j + 1) * TOPK) for j in range(4)]
                    top16([best[:, r] for r in rows], [posn[:, r].bitcast(U32) for r in rows],
                          [cand[:, j, :] for j in range(4)], TOPK * TOPK)
                b3 = t3(best, TOPK)
                TT(t3(fa, TOPK), b3, b3[:, :, 0:1].to_broadcast([P, PH, TOPK]), ALU.subtract)\
                    .then_inc(S("best_ready"), 1)
                link(TS(posa.bitcast(U32), posn.bitcast(U32), 4, None, ALU.logical_shift_right))
                link(TS(posb.bitcast(U32), posn.bitcast(U32), TOPK - 1, None, ALU.bitwise_and))
                ve.wait_ge(S("best_exp"), tb + 1)
                link(v.tensor_reduce(gsum, t3(bexp, TOPK), AX, ALU.add))
                link(v.reciprocal(grec, gsum))
                link(TT(t3(picks[:, tb, 2 * P:3 * P], TOPK), t3(bexp, TOPK),
                        grec.unsqueeze(2).to_broadcast([P, PH, TOPK]), ALU.mult))
                for half, pos in enumerate((posa, posb)):
                    link(v.tensor_copy(fb, pos.bitcast(U32)))
                    e4 = eq.rearrange("p (k c) -> p k c", c=TOPK)
                    link(TT(e4, iota[:, 0:TOPK].unsqueeze(1).to_broadcast([P, P, TOPK]),
                            fb.unsqueeze(2).to_broadcast([P, P, TOPK]), ALU.is_equal))
                    key = topf[:, tb, :].rearrange("p (h two c) -> p h two c", two=2, c=TOPK)[:, :, half, :]
                    link(TT(prod.rearrange("p (h k c) -> p h k c", h=PH, c=TOPK),
                            eq.rearrange("p (h k c) -> p h k c", h=PH, c=TOPK),
                            key.unsqueeze(2).to_broadcast([P, PH, TOPK, TOPK]), ALU.mult))
                    link(v.tensor_reduce(picks[:, tb, half * P:(half + 1) * P],
                                         prod.rearrange("p (k c) -> p k c", c=TOPK), AX, ALU.add))
                ve.sem_inc(S("picks_ready"), 1)

            def spread(u, i):
                n = i * 4 + u
                if not (isinstance(i, int) and n < 4):
                    ve.wait_ge(S("pe_done"), block_at("gate", u, i, 4).of(DONE, 4))
                rows = iota[:, :].unsqueeze(1).to_broadcast([P, 4, P])
                keys_a, keys_b, share = (
                    picksT[:, k, 4 * n:4 * n + 4] if isinstance(n, int) else
                    picksT[:, k:k + 1, bass.ds(n * 4, 4)].rearrange("p o t -> p (o t)") for k in range(3))
                v.tensor_copy(share4[:, u % 4, :], share)
                TT(t3(hot_b[:, u % 4, :], P), rows, keys_b.unsqueeze(2).to_broadcast([P, 4, P]), ALU.is_equal)
                TT(t3(hot_a[:, u % 4, :], P), rows, keys_a.unsqueeze(2).to_broadcast([P, 4, P]), ALU.is_equal)\
                    .then_inc(S("hot_ready"), 1)
            ve.wait_ge(S("picksT_ready"), NB)
            rounds(ve, T // 4, 4, spread)

            def group(i):
                ve.wait_ge(S("gates_back"), i * 16 + 16)
                step = chain(ve, S("ew_step"), i * JG)
                for k in range(JG):
                    ve.wait_ge(S("ea_ready"), i * JG + (k + 1))
                    wait(ve, S("ew_ready"), i * JG + (k - 1))
                    TT(er[:, k % 2, :], ga4[:, k % 4, :], gbuf[:, k, :], ALU.mult).then_inc(S("ew_raw"), 1)
                    ve.wait_ge(S("ew_raw"), i * JG + (k + 1))
                    split(step, ews, k, er[:, k % 2, :]).then_inc(S("ew_ready"), 1)
                for dc in range(KD):
                    tile_used(ve, tile_at("experts", (3 if dc < 4 else 4 + 3) + JG, i, 2 * JG))
                    wait(ve, S("eo_read"), i * KD)
                    TT(x[:, dc, :], x[:, dc, :], psum[:, dc, :], ALU.add).then_inc(S("eo_read"), 1)
            group(0)
            with ve.Fori(1, PK // JG) as i:
                group(i)

        @block.gpsimd
        def _(gp):
            g = nc.gpsimd
            g.memset(ones[:, :], 1.0).then_inc(S("consts_ready"), 1)
            g.iota(iota[:, :], [[1, P]], base=0, channel_multiplier=0, allow_small_or_imprecise_dtypes=True)\
                .then_inc(S("consts_ready"), 1)
            g.memset(ident[:, :], 0.0).then_inc(S("consts_ready"), 1)
            gp.wait_ge(S("consts_ready"), 3)
            g.affine_select(out=ident[:, :], in_=ident[:, :], compare_op=ALU.not_equal, fill=1.0, base=0,
                            pattern=[[-1, P]], channel_multiplier=1).then_inc(S("consts_ready"), 1)
            g.memset(maskt[:, :], 0.0).then_inc(S("mask_zero"), 1)
            gp.wait_ge(S("mask_zero"), 1)
            g.affine_select(out=maskt[:, :], in_=maskt[:, :], compare_op=ALU.is_ge, fill=NEG, base=0,
                            pattern=[[-1, P]], channel_multiplier=1).then_inc(S("mask_ready"), 1)

            def halves(stage, n, size, per=4):
                def body(u, i, size=size):
                    size = size if isinstance(size, int) else size(u)
                    a, s = tile_at(stage, u, i, per), split_at(stage, u, i, per)
                    at = (s.first % 2) * SLOT
                    tile_here(gp, a)
                    if not (isinstance(s.count, int) and s.count < 2):
                        gp.wait_ge(S("pe_done"), s.of(SPLIT_USED, 2))
                    g.tensor_tensor(wh_t[:, at:at + size], slot(a, 0, size), ones[:, 0:1].to_broadcast([P, size]),
                                    ALU.mult).then_inc(S("split_hi"), 1)
                    gp.wait_ge(S("split_hi"), s.count + 1)
                    g.tensor_tensor(wl_t[:, at:at + size], slot(a, 0, size), wh_t[:, at:at + size].bitcast(F32),
                                    ALU.subtract).then_inc(S("split_ready"), 1)
                rounds(gp, n, per, body)
            halves("rx", NR, D)
            halves("rg", NR, D)
            halves("v", 8, D)
            halves("u", HG, D)

            halves("merge", 4 * KD, lambda u: NR * P if u % 4 == 1 else D)
            halves("out", KD, D)
            for k in range(2):
                halves(f"up{k}", 2 * NFH, D)
                halves(f"down{k}", KD, SLOT)
            halves("u2", KS, D)
            for c in range(NS):
                if c >= 2:
                    tile_used(gp, tile_at("ssm", c - 2))
                gp.wait_ge(S("turned"), 2 * c + 1)
                g.tensor_tensor(ssm_s[:, 2 * (c % 2), :], st[:, 4, :], st[:, 5, :], ALU.subtract)\
                    .then_inc(S("s_ready"), 1)
                gp.wait_ge(S("turned"), 2 * c + 2)
                g.tensor_tensor(ssm_s[:, 2 * (c % 2) + 1, :], back[:, 1, :], back[:, 0, :], ALU.subtract)\
                    .then_inc(S("s_ready"), 1)
            halves("glu", 2 * KD, D)
            halves("q", KD, D)
            gp.wait_ge(S("ysg_ready"), KS)
            g.memset(sel, 0.0).then_inc(S("mask_zero"), 1)
            gp.wait_ge(S("mask_zero"), 2)
            g.affine_select(out=sel, in_=sel, compare_op=ALU.not_equal, fill=1.0, base=0,
                            pattern=[[-1, HEADS], [0, P]], channel_multiplier=1).then_inc(S("mask_ready"), 1)
            for stage, n in (("k", KD), ("v2", 8), ("ga", KD), ("out2", KD), ("query", 16)):
                halves(stage, n, D)

            def shared(u, i):
                gp.wait_ge(S("hot_ready"), i * 4 + u + 1)
                rows = t3(hot_a[:, u % 4, :], P)
                g.tensor_tensor(rows, rows, share4[:, u % 4, :].unsqueeze(2).to_broadcast([P, 4, P]), ALU.mult)\
                    .then_inc(S("hot_shared"), 1)
            rounds(gp, T // 4, 4, shared)
            halves("experts", 2 * PK, D)


HEAD_SCALE = float(P) ** -0.5


def _two_pi_parts():
    out, rest = [], TWO_PI
    for bits in (9, 11):
        scale = 2.0 ** (bits - math.ceil(math.log2(rest)))
        out.append(math.floor(rest * scale) / scale)
        rest -= out[-1]
    return out + [float(np.float32(rest))]


TWO_PI_PARTS = _two_pi_parts()


def _tiles(w):
    k, n = w.shape
    return w.reshape(k // P, P, n // P, P).transpose(2, 1, 0, 3).reshape(n // P, P, k)


def _wide_tiles(w):
    return w.reshape(4, 2, P, 2, 512).transpose(3, 0, 2, 1, 4).reshape(8, P, 1024)


def _cols(v):
    return v.reshape(-1, P).T


def kernel(**inputs):
    from concourse import bacc
    from concourse.bass_utils import run_bass_kernel_spmd

    a = {k: np.asarray(v) for k, v in inputs.items()}
    arrays = {}

    def put(name, v):
        arrays[name] = np.ascontiguousarray(v)

    xT = a["x"][0].T.reshape(KD, P, T).transpose(1, 0, 2)
    cT = a["ctx"][0].T.reshape(KD, P, TC).transpose(1, 0, 2)
    put("xT", xT)
    put("xc", np.concatenate([xT, cT], axis=2))
    wm, w_in = a["w_mod"][0], a["w_in"][0]
    put("w_moda", _tiles(wm[:, :2048]))
    put("w_modb", _tiles(wm[:, 2048:]))
    offs = np.cumsum([0, W_R, W_R, W_G, W_G, D, D])
    rx, rg, uu, vv, gr, gg = (w_in[:, lo:hi] for lo, hi in zip(offs[:-1], offs[1:]))
    put("w_rx", _tiles(rx))
    put("w_rg", _tiles(rg))
    put("w_u", _tiles(uu))
    put("w_v", _wide_tiles(vv))
    put("w_gr", _tiles(gr))
    put("w_gg", _tiles(gg))
    wa, wx = a["lru_wa"][0], a["lru_wx"][0]
    both = np.stack([wa, wx], axis=0).reshape(2, 2, 5, 2, P, 2, P)
    put("w_gates", both.transpose(1, 2, 5, 4, 0, 3, 6).reshape(2 * NR, P, 4 * P))
    put("w_sT", a["w_s"][0].transpose(2, 0, 1).reshape(P, HG * P))
    put("bsrow", np.broadcast_to(a["b_s"][0].T[None], (P, HG, P)))
    put("w_pr", _tiles(a["w_pr"][0]))
    put("w_pg", _tiles(a["w_pg"][0]))
    put("w_out", _tiles(a["w_out"][0]))
    up = a["w_up"][0]
    put("w_up", np.stack([_tiles(up[:, :D_FF]), _tiles(up[:, D_FF:])], axis=1).reshape(2 * NF, P, D))
    put("w_down", _tiles(a["w_down"][0]).reshape(KD, P, 2, SLOT).transpose(2, 0, 1, 3).reshape(2 * KD, P, SLOT))
    w2 = a["w_in_2"][0]
    o = np.cumsum([0, SSM, D, D, D, HEADS, D, D])
    wu, wq, wk, wv, wf, wgs, wga = (w2[:, lo:hi] for lo, hi in zip(o[:-1], o[1:]))
    put("w_u2", _tiles(wu))
    put("w_q", _tiles(wq))
    put("w_k", _tiles(wk))
    put("w_v2", _wide_tiles(wv))
    put("w_f", wf.reshape(KD, P, HEADS).transpose(1, 0, 2).reshape(P, KD * HEADS))
    put("w_ga", _tiles(wga))
    glu = a["ssm_w_glu_2"][0]
    vg = np.concatenate([_tiles(glu[:, :D]), _tiles(glu[:, D:])], axis=2)
    put("w_glu", np.stack([vg, _tiles(wgs)], axis=1).reshape(2 * KD, P, D))
    put("w_out2", _tiles(a["w_out_2"][0]))
    put("w_query", _tiles(a["peer_w_query_2"][0]))
    sk = a["peer_sub_keys_2"][0].reshape(16, PK, P)
    put("w_keys", sk.transpose(2, 0, 1).reshape(P, 2, 8 * P).transpose(1, 0, 2))
    ssm = np.zeros((NS, P, 4, P), np.float32)
    for k, name in enumerate(("ssm_b_re_2", "ssm_b_im_2", "ssm_c_re_2", "ssm_c_im_2")):
        w = a[name][0] if k < 2 else a[name][0].transpose(0, 2, 1)
        for g in range(32):
            c, r = g // 2, g % 2
            f0 = 32 * (c % 4) + 16 * r
            ssm[c, 64 * r:64 * r + 64, k, f0:f0 + 16] = w[g]
    put("w_ssm", ssm.reshape(NS, P, 4 * P))
    ut = a["peer_u_2"][0].reshape(PK, PK // JG, JG, KD, P).transpose(1, 2, 4, 3, 0).reshape(-1, JG, P, D)
    vt = a["peer_v_2"][0].reshape(PK, PK // JG, JG // 2, 2, 2, 512).transpose(1, 4, 2, 0, 3, 5)
    put("tables", np.concatenate([ut, vt.reshape(-1, JG, P, D)], axis=1).reshape(-1, P, D))

    v = {"c2": np.stack([a["c"][0].reshape(KD, P), a["c_ctx"].reshape(KD, P)], axis=1).reshape(16, P).T,
         "bmod": _cols(a["b_mod"][0]), "g1": _cols(a["g_norm1"][0]),
         "convw": a["conv_w"][0].reshape(KR, NR, P).transpose(2, 1, 0).reshape(P, NR * KR),
         "convb": _cols(a["conv_b"][0]), "lam": _cols(a["lru_lam"][0].reshape(-1)),
         "ba": _cols(a["lru_ba"][0].reshape(-1)), "bx": _cols(a["lru_bx"][0].reshape(-1)),
         "gv": _cols(a["g_v"][0]), "g2": _cols(a["g_norm2"][0]),
         "fcw": a["ffn_conv_w"][0].reshape(9, NF, P).transpose(2, 1, 0).reshape(P, NF * 9),
         "fcb": _cols(a["ffn_conv_b"][0]), "gfin": _cols(a["g_final"]), "mixg": _cols(a["mix_norm_g_2"][0]),
         "are": _cols(a["ssm_a_re_2"][0].reshape(-1)), "aim": _cols(a["ssm_a_im_2"][0].reshape(-1)),
         "lstep": _cols(np.repeat(a["ssm_log_step_2"][0], 64)), "dskip": _cols(a["ssm_d_2"][0]),
         "fbias": np.concatenate([a["fox_forget_bias_2"][0], np.zeros(P - HEADS, np.float32)])[:, None],
         "qg": a["q_norm_g_2"][0][:, None], "kg": a["k_norm_g_2"][0][:, None], "ffng": _cols(a["ffn_norm_g_2"][0]),
         "eps": np.full((P, 1), EPS, np.float32)}
    put("vecs", np.concatenate([v[n] for n, _ in VECS], axis=1))

    nc = bacc.Bacc("TRN2", target_bir_lowering=False, num_devices=1)
    io = {k: nc.dram_tensor(k, w.shape, F32, kind="ExternalInput").ap() for k, w in arrays.items()}
    io["out"] = nc.dram_tensor("out", (D, T), F32, kind="ExternalOutput").ap()
    build(nc, io)
    r = run_bass_kernel_spmd(nc, [arrays], core_ids=[0])
    return r.results[0]["out"].T.reshape(1, T, D)
```
